# Optimizing a Trainium2 kernel written in Bass

```python
import math
import jax, jax.numpy as jnp
from jax import lax
import numpy as np

D_MODEL = 1024
BATCH = 1
SEQ = 512
DEPTH = 2

SSM_EXPAND = 2
SSM_D_INNER = SSM_EXPAND * D_MODEL
SSM_HEAD_DIM = 64
SSM_HEADS = SSM_D_INNER // SSM_HEAD_DIM
SSM_GROUPS = 4
SSM_STATE = 128
SSM_CONV = 4
SSM_CHUNK = 128
SSM_CONV_DIM = SSM_D_INNER + 2 * SSM_GROUPS * SSM_STATE

DIFF_HEADS = 8
DIFF_HEAD_DIM = 64
DIFF_QK_WIDTH = DIFF_HEADS * 2 * DIFF_HEAD_DIM
DIFF_V_WIDTH = DIFF_HEADS * 2 * DIFF_HEAD_DIM
ATTN_BLOCK = 128
ROPE_THETA = 10000.0

D_FF = 4 * D_MODEL
N_ADA = 6
EPS = 1e-5

IN_PROJ_WIDTHS = (SSM_D_INNER, SSM_CONV_DIM, SSM_HEADS, DIFF_QK_WIDTH, DIFF_QK_WIDTH, DIFF_V_WIDTH, D_MODEL, D_MODEL)
IN_PROJ_WIDTH = sum(IN_PROJ_WIDTHS)

kernel_name = "hybrid_ssd_diffattn_gated_block"

def split_cols(t, widths):
    idx = []
    acc = 0
    for w in widths[:-1]:
        acc += w
        idx.append(acc)
    return jnp.split(t, idx, axis=-1)

def rms_norm(x, gain):
    xf = x.astype(jnp.float32)
    y = xf * lax.rsqrt(jnp.mean(xf * xf, axis=-1, keepdims=True) + EPS)
    return (y * gain.astype(jnp.float32)).astype(x.dtype)

def lambda_init_fn(layer_idx):
    return 0.8 - 0.6 * math.exp(-0.3 * layer_idx)

def rope_tables(seq, dim):
    inv = 1.0 / (ROPE_THETA ** (jnp.arange(0, dim, 2, dtype=jnp.float32) / dim))
    ang = jnp.arange(seq, dtype=jnp.float32)[:, None] * inv[None, :]
    return jnp.cos(ang), jnp.sin(ang)

def apply_rope(t, cos, sin):
    half = t.shape[-1] // 2
    cos = cos[None, :, None, None, :]
    sin = sin[None, :, None, None, :]
    tf = t.astype(jnp.float32)
    t1, t2 = tf[..., :half], tf[..., half:]
    return jnp.concatenate([t1 * cos - t2 * sin, t2 * cos + t1 * sin], axis=-1).astype(t.dtype)

def causal_dwconv(x, w, b):
    k = w.shape[0]
    y = lax.conv_general_dilated(
        x, w[:, None, :].astype(x.dtype), window_strides=(1,), padding=[(k - 1, 0)],
        dimension_numbers=("NWC", "WIO", "NWC"), feature_group_count=x.shape[-1])
    return y + b.astype(x.dtype)

def ssd_chunked(xh, dt, a, bm, cm):
    bsz, s, h, p = xh.shape
    g, n = bm.shape[-2], bm.shape[-1]
    r = h // g
    nc, l = s // SSM_CHUNK, SSM_CHUNK
    X = (xh * dt[..., None]).reshape(bsz, nc, l, g, r, p)
    a_step = (dt * a).reshape(bsz, nc, l, g, r)
    Bc = bm.reshape(bsz, nc, l, g, n)
    Cc = cm.reshape(bsz, nc, l, g, n)
    a_cum = jnp.cumsum(a_step, axis=2)
    causal = jnp.tril(jnp.ones((l, l), dtype=bool))[None, None, :, :, None, None]
    seg = a_cum[:, :, :, None] - a_cum[:, :, None, :]
    decay = jnp.exp(jnp.where(causal, seg, -jnp.inf))
    cb = jnp.einsum("bclgn,bcsgn->bclsg", Cc, Bc)
    y_diag = jnp.einsum("bclsgr,bcsgrp->bclgrp", cb[..., None] * decay, X)
    decay_to_end = jnp.exp(a_cum[:, :, -1:] - a_cum)
    states = jnp.einsum("bclgn,bclgrp->bcgrpn", Bc, X * decay_to_end[..., None])
    chunk_decay = jnp.exp(a_cum[:, :, -1])

    def step(hstate, inp):
        s_c, d_c = inp
        return hstate * d_c[..., None, None] + s_c, hstate

    h0 = jnp.zeros((bsz, g, r, p, n), dtype=X.dtype)
    _, prev = lax.scan(step, h0, (jnp.moveaxis(states, 1, 0), jnp.moveaxis(chunk_decay, 1, 0)))
    prev = jnp.moveaxis(prev, 0, 1)
    y_off = jnp.einsum("bclgn,bcgrpn->bclgrp", Cc, prev) * jnp.exp(a_cum)[..., None]
    return (y_diag + y_off).reshape(bsz, s, h, p)

def mamba2_branch(z, xbc, dt_raw, conv_w, conv_b, dt_bias, a_log, d_skip, norm_g):
    bsz, s, _ = z.shape
    xbc = jax.nn.silu(causal_dwconv(xbc, conv_w, conv_b))
    xs, bm, cm = split_cols(xbc, (SSM_D_INNER, SSM_GROUPS * SSM_STATE, SSM_GROUPS * SSM_STATE))
    xh = xs.reshape(bsz, s, SSM_HEADS, SSM_HEAD_DIM).astype(jnp.float32)
    bm = bm.reshape(bsz, s, SSM_GROUPS, SSM_STATE).astype(jnp.float32)
    cm = cm.reshape(bsz, s, SSM_GROUPS, SSM_STATE).astype(jnp.float32)
    dt = jax.nn.softplus(dt_raw.astype(jnp.float32) + dt_bias.astype(jnp.float32))
    a = -jnp.exp(a_log.astype(jnp.float32))
    y = ssd_chunked(xh, dt, a, bm, cm) + d_skip.astype(jnp.float32)[:, None] * xh
    y = y.reshape(bsz, s, SSM_D_INNER) * jax.nn.silu(z.astype(jnp.float32))
    yg = y.reshape(bsz, s, SSM_GROUPS, SSM_D_INNER // SSM_GROUPS)
    yg = yg * lax.rsqrt(jnp.mean(yg * yg, axis=-1, keepdims=True) + EPS)
    y = yg.reshape(bsz, s, SSM_D_INNER) * norm_g.astype(jnp.float32)
    return y.astype(z.dtype)

def diff_attention_branch(q, k, v, cos, sin, lam_q1, lam_k1, lam_q2, lam_k2, subln_g, lambda_init):
    bsz, s, _ = q.shape
    h, d = DIFF_HEADS, DIFF_HEAD_DIM
    nb = s // ATTN_BLOCK
    q = apply_rope(q.reshape(bsz, s, h, 2, d), cos, sin)
    k = apply_rope(k.reshape(bsz, s, h, 2, d), cos, sin)
    v = v.reshape(bsz, s, h, 2 * d)
    lam = (jnp.exp(jnp.sum(lam_q1.astype(jnp.float32) * lam_k1.astype(jnp.float32)))
           - jnp.exp(jnp.sum(lam_q2.astype(jnp.float32) * lam_k2.astype(jnp.float32)))
           + lambda_init)
    qb = q.reshape(bsz, nb, ATTN_BLOCK, h, 2, d).transpose(1, 0, 3, 4, 2, 5)
    kt = k.transpose(0, 2, 3, 1, 4)
    vt = v.transpose(0, 2, 1, 3)
    key_pos = jnp.arange(s)
    scale = d ** -0.5

    def block(args):
        q_blk, start = args
        sc = jnp.einsum("bhiqd,bhikd->bhiqk", q_blk, kt).astype(jnp.float32) * scale
        q_pos = start + jnp.arange(ATTN_BLOCK)
        mask = key_pos[None, :] <= q_pos[:, None]
        pr = jax.nn.softmax(jnp.where(mask, sc, -jnp.inf), axis=-1)
        attn = pr[:, :, 0] - lam * pr[:, :, 1]
        return jnp.einsum("bhqk,bhkv->bhqv", attn.astype(vt.dtype), vt)

    starts = jnp.arange(nb) * ATTN_BLOCK
    o = lax.map(block, (qb, starts))
    o = o.transpose(1, 0, 3, 2, 4).reshape(bsz, s, h, 2 * d)
    o = rms_norm(o, subln_g) * (1.0 - lambda_init)
    return o.reshape(bsz, s, h * 2 * d)

def setup_inputs(seed: int = 0) -> dict:
    key = jax.random.key(seed)
    ks = jax.random.split(key, 32)
    f32 = jnp.float32
    L = DEPTH

    def nrm(k, shape, scale):
        return jax.random.normal(k, shape, f32) * scale

    u_dt = jax.random.uniform(ks[10], (L, SSM_HEADS), f32)
    dt0 = jnp.exp(u_dt * (math.log(0.1) - math.log(0.001)) + math.log(0.001))
    dt_bias = dt0 + jnp.log(-jnp.expm1(-dt0))
    a0 = jax.random.uniform(ks[11], (L, SSM_HEADS), f32, 1.0, 16.0)
    return {
        "x": nrm(ks[0], (BATCH, SEQ, D_MODEL), 1.0),
        "c": nrm(ks[1], (BATCH, D_MODEL), 1.0),
        "w_ada": nrm(ks[2], (L, D_MODEL, N_ADA * D_MODEL), 0.5 * D_MODEL ** -0.5),
        "b_ada": nrm(ks[3], (L, N_ADA * D_MODEL), 0.02),
        "norm1_g": 1.0 + nrm(ks[4], (L, D_MODEL), 0.05),
        "w_in": nrm(ks[5], (L, D_MODEL, IN_PROJ_WIDTH), D_MODEL ** -0.5),
        "conv_w": nrm(ks[6], (L, SSM_CONV, SSM_CONV_DIM), SSM_CONV ** -0.5),
        "conv_b": nrm(ks[7], (L, SSM_CONV_DIM), 0.02),
        "dt_bias": dt_bias,
        "a_log": jnp.log(a0),
        "d_skip": 1.0 + nrm(ks[12], (L, SSM_HEADS), 0.1),
        "ssm_norm_g": 1.0 + nrm(ks[13], (L, SSM_D_INNER), 0.05),
        "lam_q1": nrm(ks[14], (L, DIFF_HEAD_DIM), 0.1),
        "lam_k1": nrm(ks[15], (L, DIFF_HEAD_DIM), 0.1),
        "lam_q2": nrm(ks[16], (L, DIFF_HEAD_DIM), 0.1),
        "lam_k2": nrm(ks[17], (L, DIFF_HEAD_DIM), 0.1),
        "subln_g": 1.0 + nrm(ks[18], (L, 2 * DIFF_HEAD_DIM), 0.05),
        "w_ssm_out": nrm(ks[19], (L, SSM_D_INNER, D_MODEL), SSM_D_INNER ** -0.5),
        "w_attn_out": nrm(ks[20], (L, DIFF_V_WIDTH, D_MODEL), DIFF_V_WIDTH ** -0.5),
        "w_out": nrm(ks[21], (L, D_MODEL, D_MODEL), D_MODEL ** -0.5),
        "norm2_g": 1.0 + nrm(ks[22], (L, D_MODEL), 0.05),
        "w_ff1": nrm(ks[23], (L, D_MODEL, D_FF), D_MODEL ** -0.5),
        "w_ff2": nrm(ks[24], (L, D_FF, D_MODEL), D_FF ** -0.5),
        "final_g": 1.0 + nrm(ks[25], (D_MODEL,), 0.05),
    }

def reference(x, c, w_ada, b_ada, norm1_g, w_in, conv_w, conv_b, dt_bias, a_log, d_skip,
              ssm_norm_g, lam_q1, lam_k1, lam_q2, lam_k2, subln_g, w_ssm_out, w_attn_out,
              w_out, norm2_g, w_ff1, w_ff2, final_g):
    s = x.shape[1]
    cos, sin = rope_tables(s, DIFF_HEAD_DIM)
    c_act = jax.nn.silu(c)
    for l in range(DEPTH):
        ada = c_act @ w_ada[l] + b_ada[l]
        sh1, sc1, g1, sh2, sc2, g2 = jnp.split(ada, N_ADA, axis=-1)
        h = rms_norm(x, norm1_g[l]) * (1.0 + sc1[:, None]) + sh1[:, None]
        proj = h @ w_in[l]
        z, xbc, dt_raw, q, k, v, gate_s, gate_a = split_cols(proj, IN_PROJ_WIDTHS)
        y_ssm = mamba2_branch(z, xbc, dt_raw, conv_w[l], conv_b[l], dt_bias[l], a_log[l],
                              d_skip[l], ssm_norm_g[l]) @ w_ssm_out[l]
        y_att = diff_attention_branch(q, k, v, cos, sin, lam_q1[l], lam_k1[l], lam_q2[l],
                                      lam_k2[l], subln_g[l], lambda_init_fn(l)) @ w_attn_out[l]
        mixed = jax.nn.sigmoid(gate_s) * y_ssm + jax.nn.sigmoid(gate_a) * y_att
        x = x + g1[:, None] * (mixed @ w_out[l])
        h = rms_norm(x, norm2_g[l]) * (1.0 + sc2[:, None]) + sh2[:, None]
        u = jnp.square(jax.nn.relu(h @ w_ff1[l]))
        x = x + g2[:, None] * (u @ w_ff2[l])
    return rms_norm(x, final_g)


_drawn_inputs = setup_inputs


def setup_inputs(seed=0):
    import zlib

    import numpy as np

    out = dict(_drawn_inputs(seed))
    spreads = {}
    factors = {'norm1_g': 2.825,
     'conv_b': 8.0,
     'd_skip': 22.428,
     'ssm_norm_g': 4.93,
     'lam_q1': 3.178,
     'lam_k1': 3.831,
     'lam_q2': 3.069,
     'lam_k2': 4.256,
     'subln_g': 6.879}
    for name, (base, spread) in spreads.items():
        noise = np.random.default_rng([zlib.crc32(name.encode()), seed]).standard_normal(out[name].shape)
        drawn = base * np.exp(spread * noise) if base else spread * noise
        out[name] = __import__('jax').numpy.asarray(drawn.astype(out[name].dtype))
    for name, factor in factors.items():
        out[name] = (out[name] * factor).astype(out[name].dtype)
    return out
```

```python
from contextlib import ExitStack

import numpy as np

import concourse.bass as bass
from concourse import mybir

F32 = mybir.dt.float32
F32R = mybir.dt.float32r
ALU = mybir.AluOpType
ACT = mybir.ActivationFunctionType
AX_X = mybir.AxisListType.X

P = 128
DEPTH, D, S = 2, 1024, 512
KB = D // P
TB = S // P
DI = 2 * D
GROUPS, STATE, HD = 4, 128, 64
HEADS = DI // HD
HG = HEADS // GROUPS
GW = DI // GROUPS
AH, AD = 8, 64
FF = 4 * D
CONV = 4
CONV_BLOCKS = (DI + 2 * GROUPS * STATE) // P
EPS = 1e-5
UW = 256

N_BC, N_XS, N_GATE, N_ZS, N_QKV, N_AO, N_WO, N_FF = 4, 8, 8, 16, 12, 4, 4, 32
U_BC = 0
U_XS = U_BC + N_BC
U_GATE = U_XS + N_XS
U_ZS = U_GATE + N_GATE
U_QKV = U_ZS + N_ZS
U_AO = U_QKV + N_QKV
U_WO = U_AO + N_AO
U_FF = U_WO + N_WO
UNITS = U_FF + N_FF
ADA = 6 * D // UW
PIECES = ADA + UNITS
ADA_H, PIECES_H, UNITS_H = ADA // 2, PIECES // 2, UNITS // 2

C_N1, C_CW, C_CB = 0, 8, 8 + CONV * CONV_BLOCKS
C_DSK = C_CB + CONV_BLOCKS
C_SNG = C_DSK + HEADS
C_SUB = C_SNG + DI // P
C_LAM = C_SUB + 1
C_BADA = C_LAM + 4 * AD
C_N2 = C_BADA + 6 * KB
C_DTB = C_N2 + KB
C_ALOG = C_DTB + 1
C_LI = C_ALOG + 1
C_OML = C_LI + 1
NPAR = C_OML + 1
K_C, K_FG, K_ID = 0, KB, 2 * KB
K_TRI, K_NEG = K_ID + P, K_ID + 2 * P
K_SEL = K_NEG + P
NCON = K_SEL + HEADS

NORM = {"sq": 8, "sq_used": 8, "ss": 1, "ms": 1, "rs": 1, "pre": 8, "h_hi": 8, "h_lo": 8, "bank0": 1, "bank1": 1}
PHASES = [
    ("start", 1, {**NORM, "bank2": 1, "bank3": 1, "bank0": 2, "lam": 2, "dtw": 2, "dt_a": 2, "dt_v": 1, "x_tok": 1}),
    ("bc", 2, {"seed": 4, "taps": 4, "tanh": 4, "silu": 4}),
    ("xs", 4, {"seed": 4, "taps": 4, "tanh": 4, "silu": 4, "bank0": 2, "bank1": 2}),
    ("ssd", 4, {"bc_copy": 1, "cb": 1, "b_tok": 1, "bank0": 8, "bank1": 5, "bank2": 4, "bank3": 4, "seg": 8,
                "sum": 8, "cdec": 1, "m": 8, "m_used": 8, "xd": 3, "state": 3, "y": 1}),
    ("z", 2, {"z_act": 8, "z_used": 9, "y_gate": 2, "y_sq": 2, "y_ms": 2, "y_rs": 2, "yn": 8,
              "y_hi": 8, "y_lo": 8, "bank0": 4, "bank1": 4}),
    ("att", 2, {"swap": 8, "rope": 8, "v": 2, "bank0": 16, "bank1": 16, "bank2": 20, "bank3": 4,
                "mx": 16, "e": 16, "p": 16, "pt": 16, "o_sq": 4, "o_ms": 4, "o_rs": 4, "on": 4, "o_hi": 4,
                "o_lo": 4}),
    ("mix", 1, {**NORM, "mixed": 1, "x_sum": 1, "mix_hi": 8, "mix_lo": 8}),
    ("ff", 4, {"relu": 8, "u_hi": 8, "u_lo": 8}),
    ("end", 1, {"layer": 1}),
]
TOTAL, BASE = {}, {}
for _phase, _rounds, _signals in PHASES:
    for _name, _n in _signals.items():
        BASE[_phase, _name] = TOTAL.get(_name, 0)
        TOTAL[_name] = TOTAL.get(_name, 0) + _rounds * _n
PER = {phase: signals for phase, _, signals in PHASES}


class Step:

    def __init__(self, layer, phase, i=0):
        self.layer, self.phase, self.i, self.seen = layer, phase, i, {}

    def __call__(self, name):
        k = self.seen.get(name, 0)
        self.seen[name] = k + 1
        return self.at(name, k)

    def at(self, name, k):
        per = PER[self.phase][name]
        base = BASE[self.phase, name]
        if isinstance(self.i, int):
            return self.layer * TOTAL[name] + (base + self.i * per + k)
        return self.layer * TOTAL[name] + self.i * per + (base + k)

    def end(self):
        for name, k in self.seen.items():
            assert k == PER[self.phase][name], (self.phase, name, k)


def wait(eng, sem, value):
    eng.wait_ge(sem, value)


def build(nc, stream, dtw, params, consts, ropes, xT, xsave, out):
    ctx = ExitStack()
    with ctx:
        at = [nc.sbuf_base + (-nc.sbuf_base) % 32]
        fence = ctx.enter_context(nc.sbuf_tensor("fence", [P, 212000 // 4], F32))
        del fence

        def place(name, shape, dt, offset):
            return nc.alloc_sbuf_tensor_at(name, shape, dt, offset=offset)

        def region(nbytes):
            o = at[0]
            at[0] += nbytes + (-nbytes) % 32
            return o

        K16 = KB * S * 4
        T2 = S * 4
        r_raw, r_hi, r_lo = region(K16), region(K16), region(K16)
        raw = place("raw", [P, 2, KB, UW], F32, r_raw)
        w_hi = place("w_hi", [P, 2, KB, UW], F32R, r_hi)
        w_lo = place("w_lo", [P, 2, KB, UW], F32R, r_lo)
        h_hi = place("h_hi", [P, KB, S], F32R, region(K16))
        h_lo = place("h_lo", [P, KB, S], F32R, region(K16))
        r_op = region(2 * K16)
        op_hi = place("op_hi", [P, KB, S], F32R, r_op)
        op_lo = place("op_lo", [P, KB, S], F32R, r_op + K16)
        r_x = region(K16)
        bct = place("bct", [P, 2 * GROUPS, S], F32, r_x)
        mix = place("mix", [P, KB, S], F32, r_x)
        r_a = region(2 * K16)
        y_tok = place("y_tok", [P, TB, DI], F32, r_a)
        x = place("x", [P, KB, S], F32, r_a + K16)
        r_g = region(2 * K16)
        gates = place("gates", [P, 2 * KB, S], F32, r_g)
        gate_s, gate_a = gates[:, 0:KB], gates[:, KB:2 * KB]

        sq = place("sq", [P, 2, S], F32, r_op)
        ss = place("ss", [P, S], F32, r_op + 2 * T2)
        pre = place("pre", [P, 2, S], F32, r_op + 3 * T2)
        conv = place("conv", [P, 4, S], F32, r_op)
        ctanh = place("ctanh", [P, 4, S], F32, r_op + 4 * T2)
        xsf = place("xsf", [P, 4, S], F32, r_op + 8 * T2)
        bg = place("bg", [P, S], F32, r_op)
        cg = place("cg", [P, S], F32, r_op + T2)
        b_tok = place("b_tok", [P, TB, STATE], F32, r_op + 2 * T2)
        cbm = place("cbm", [P, TB, P], F32, r_op + 3 * T2)
        decayed = place("decayed", [P, 2, TB, P], F32, r_op + 4 * T2)
        xdt = place("xdt", [P, TB, GW], F32, r_op + 6 * T2)
        xd = place("xd", [P, TB - 1, GW], F32, r_op + 10 * T2)
        state = place("state", [P, 2, GW], F32, r_op + 13 * T2)
        y_off = place("y_off", [P, GW], F32, r_op + 15 * T2)

        ada_acc = place("ada_acc", [P, 2, UW], F32, r_g)
        dtw_raw = place("dtw_raw", [P, KB, P], F32, r_g + T2)
        dtw_hi = place("dtw_hi", [P, KB, P], F32R, r_g + 3 * T2)
        dtw_lo = place("dtw_lo", [P, KB, P], F32R, r_g + 5 * T2)
        dt_x = place("dt_x", [HEADS, S], F32, r_g + 7 * T2)
        dt_e = place("dt_e", [HEADS, S], F32, r_g + 8 * T2)
        dt_s = place("dt_s", [HEADS, S], F32, r_g + 9 * T2)
        dt_s2 = place("dt_s2", [HEADS, S], F32, r_g + 10 * T2)
        dt_p = place("dt_p", [HEADS, S], F32, r_g + 11 * T2)
        dt_one = place("dt_one", [HEADS, S], F32, r_g + 12 * T2)
        dt_cum = place("dt_cum", [HEADS, S], F32, r_g + 13 * T2)
        dt_rows = place("dt_rows", [3 * HEADS, S], F32, r_g + 14 * T2)

        qT = place("qT", [P, 2, S], F32, r_a)
        kT = place("kT", [P, 2, S], F32, r_a + 2 * T2)
        v_tok = place("v_tok", [P, TB, UW], F32, r_a + 4 * T2)
        swap = place("swap", [P, S], F32, r_a + 6 * T2)
        qc = place("qc", [P, S], F32, r_a + 7 * T2)
        probs = place("probs", [P, 2, 2, S], F32, r_g)
        probsT = place("probsT", [P, 2, S], F32, r_g + 4 * T2)
        o_n = place("o_n", [P, TB, P], F32, r_g + 6 * T2)
        relu = place("relu", [P, 4, S], F32, r_g)
        usq = place("usq", [P, 2, S], F32, r_g + 4 * T2)
        y_out = place("y_out", [P, KB, S], F32, r_g + K16)

        r_z = region(3 * T2)
        zt = place("zt", [P, 2, UW], F32, r_z)
        zh = place("zh", [P, 2, UW], F32, r_z + T2)
        yn = place("yn", [P, TB, P], F32, r_z + 2 * T2)
        seg = place("seg", [P, 2, TB, P], F32, r_z)
        rope_cos = place("rope_cos", [P, S], F32, r_z)
        rope_sin = place("rope_sin", [P, S], F32, r_z + T2)

        def small(name, cols, dt=F32, rows=P):
            return place(name, [rows, cols], dt, region(cols * 4))

        con = small("con", NCON)
        par = small("par", NPAR)
        ident = con[:, K_ID:K_ID + P]
        first = small("first", 2 + 3 * KB)
        ones, cact, g1h = first[:, 0:2], first[:, 2:2 + 2 * KB], first[:, 2 + 2 * KB:2 + 3 * KB]
        ada = small("ada", 6 * KB)
        ada_v = ada[:, :].rearrange("p (a k) -> p a k", a=6)
        cw = small("cw", (CONV + 1) * CONV_BLOCKS)
        amul = small("amul", 2 * KB)
        lamw = small("lamw", 2 * AD)
        odd = small("odd", 8)
        lams, a_neg, subg = odd[:, 0:4], odd[:, 4:6], odd[:, 6:7]
        acum = small("acum", S, F32R, 2 * HEADS)
        selg = small("selg", HG, F32R, 2 * HEADS)
        tok = place("tok", [P, TB, 3 * HEADS], F32, region(TB * 3 * HEADS * 4))
        ea_tok = place("ea_tok", [P, TB, HEADS], F32, region(TB * HEADS * 4))
        dec_tok = place("dec_tok", [P, TB, HEADS], F32, region(TB * HEADS * 4))
        cdec = place("cdec", [P, HG, TB], F32, region(HG * TB * 4))
        smalls = small("smalls", 9 * 4)
        ms, rs, y_ms, y_rs, half,\
            mxs, mxn, den, rden = (smalls[:, 4 * n:4 * n + 4] for n in range(9))
        assert at[0] <= nc.sbuf_usable_end, (at[0], nc.sbuf_usable_end)

        def ps(name):
            return ctx.enter_context(nc.psum_tensor(name, [P, S], F32))

        gb = [ps(f"gemm{b}") for b in range(4)]
        ab = [ps(f"aux{b}") for b in range(4)]

        def sem(name):
            return ctx.enter_context(nc.semaphore(name))

        raw_in = [sem("raw_in0"), sem("raw_in1")]
        hi_ready, lo_ready = sem("hi_ready"), sem("lo_ready")
        gemm_done = sem("gemm_done")
        bank_free = [sem("bank_free0"), sem("bank_free1")]
        aux_full = [sem(f"aux_full{b}") for b in range(4)]
        aux_free = [sem(f"aux_free{b}") for b in range(4)]
        ada_step, ada_out = sem("ada_step"), sem("ada_out")
        con_in, par_in, dtw_in, x_in = sem("con_in"), sem("par_in"), sem("dtw_in"), sem("x_in")
        x_saved, x_back, rope_in, out_done = sem("x_saved"), sem("x_back"), sem("rope_in"), sem("out_done")
        ready = sem("ready")
        c_tanh, cact_ready = sem("c_tanh"), sem("cact_ready")
        S_ = {name: sem("s_" + name) for name in TOTAL if not name.startswith("bank")}

        LO_CREDIT, DONE_CREDIT, BANK_CREDIT, AUX_CREDIT, LAYER_CREDIT = 1, 4, 2, 1, 1
        SILU_CREDIT, U_CREDIT, ROPE_CREDIT, Z_CREDIT, Y_CREDIT = 4, 4, 1, 1, 1

        def done_at(l, n, j):
            return l * (2 * UNITS) + n * 2 + (j + 1 + DONE_CREDIT)

        def raw_at(l, nh):
            return (l * PIECES_H + nh + 1) * 16

        def sp_program(sp):
            sp.dma_start(con[:], consts).then_inc(con_in, 16)
            sp.dma_start(x[:], xT).then_inc(x_in, 16)
            with sp.Fori(0, DEPTH) as l:
                wait(sp, S_["layer"], l + LAYER_CREDIT)
                sp.dma_start(par[:], params[bass.ds(l, 1)].rearrange("l p n -> p (l n)")).then_inc(par_in, 16)
                sp.dma_start(dtw_raw[:], dtw[bass.ds(l, 1)].rearrange("l p (k n) -> p (l k) n", k=KB)).then_inc(dtw_in, 16)
                wait(sp, x_in, 16)
                sp.dma_start(xsave, x[:]).then_inc(x_saved, 16)

                def load(piece, slot):
                    sp.dma_start(raw[:, slot], stream[bass.ds(l * PIECES + piece, 1)].rearrange(
                        "u p (k n) -> p (u k) n", k=KB)).then_inc(raw_in[slot], 16)

                for slot in range(2):
                    wait(sp, lo_ready, l * UNITS + LO_CREDIT)
                    load(slot, slot)
                with sp.Fori(1, ADA_H) as i:
                    for slot in range(2):
                        wait(sp, ada_step, l * (ADA * KB) + (i * 2 + (slot - 1)) * KB)
                        load(i * 2 + slot, slot)
                for slot in range(2):
                    wait(sp, ada_step, l * (ADA * KB) + (ADA - 1 + slot) * KB)
                    load(ADA + slot, slot)

                def units(i):
                    for slot in range(2):
                        wait(sp, lo_ready, l * UNITS + i * 2 + (slot - 1 + LO_CREDIT))
                        load(i * 2 + (ADA + slot), slot)

                with sp.Fori(1, U_QKV // 2 + 1) as i:
                    units(i)
                wait(sp, S_["yn"], PHASES_AT(l, "z", "yn", 2 * 8))
                sp.dma_start(x[:], xsave).then_inc(x_back, 16)
                wait(sp, S_["z_used"], PHASES_AT(l, "z", "z_used", 2 * 9 + Z_CREDIT))
                sp.dma_start(rope_cos[:], ropes[0]).then_inc(rope_in, 16)
                sp.dma_start(rope_sin[:], ropes[1]).then_inc(rope_in, 16)
                with sp.Fori(U_QKV // 2 + 1, UNITS_H) as i:
                    units(i)
            wait(sp, S_["pre"], DEPTH * TOTAL["pre"] + KB)
            sp.dma_start(out, y_out[:]).then_inc(out_done, 16)
            sp.wait_ge(out_done, 16)

        def PHASES_AT(l, phase, name, k):
            return l * TOTAL[name] + (BASE[phase, name] + k)

        def pe_program(pe):
            mm = nc.tensor.matmul
            pe.sem_inc(gemm_done, DONE_CREDIT)
            pe.wait_ge(con_in, 16)
            pe.wait_ge(ready, 1)

            def aux(step, b, off=0):
                pe.wait_ge(aux_free[b], step(f"bank{b}") + AUX_CREDIT)
                return ab[b]

            def unit_wait(l, n, slot):
                pe.wait_ge(lo_ready, l * UNITS + n + (1 + LO_CREDIT))
                nh = (n - slot) // 2 if isinstance(n, int) else None
                return nh

            def open_unit(l, nh, slot):
                pe.wait_ge(lo_ready, l * UNITS + nh * 2 + (slot + 1 + LO_CREDIT))
                pe.wait_ge(bank_free[slot], (l * UNITS_H + nh) * 2 + BANK_CREDIT)

            def unit(l, nh, slot, hi, lo, ready_k=None):
                open_unit(l, nh, slot)
                for k in range(KB):
                    if ready_k:
                        ready_k(k)
                    for j in range(2):
                        o = gb[2 * slot + j][:]
                        cols = slice(j * P, (j + 1) * P)
                        mm(o, w_hi[:, slot, k, cols], hi[:, k, :], start=k == 0, stop=False)
                        mm(o, w_hi[:, slot, k, cols], lo[:, k, :], start=False, stop=False)
                        last = mm(o, w_lo[:, slot, k, cols], hi[:, k, :], start=False, stop=k == KB - 1)
                        if k == KB - 1:
                            last.then_inc(gemm_done, 1)

            def unit_tok(l, nh, slot):
                open_unit(l, nh, slot)
                for t in range(TB):
                    o = gb[2 * slot + t // 2][:, (t % 2) * UW:(t % 2 + 1) * UW]
                    toks = slice(t * P, (t + 1) * P)
                    for k in range(KB):
                        mm(o, h_hi[:, k, toks], w_hi[:, slot, k, :], start=k == 0, stop=False)
                        mm(o, h_lo[:, k, toks], w_hi[:, slot, k, :], start=False, stop=False)
                        last = mm(o, h_hi[:, k, toks], w_lo[:, slot, k, :], start=False, stop=k == KB - 1)
                    if t % 2:
                        last.then_inc(gemm_done, 1)

            def transposes(bank, source, rows=P, cols=P, n=TB):
                for t in range(n):
                    last = nc.tensor.transpose(bank[0:cols, t * P:t * P + rows], source(t), ident[0:rows, 0:rows])
                return last

            def norm(step):
                pe.wait_ge(S_["ss"], step("ss") + 1)
                b = aux(step, 0)
                for t in range(TB):
                    last = mm(b[:, t:t + 1], ss[:, t * P:(t + 1) * P], ones[:, 0:1], start=True, stop=True)
                last.then_inc(aux_full[0], 1)
                pe.wait_ge(S_["rs"], step("rs") + 1)
                b = aux(step, 1)
                for t in range(TB):
                    last = mm(b[:, t * P:(t + 1) * P], rs[:, t:t + 1].broadcast_to([P, P]), ident, start=True, stop=True)
                last.then_inc(aux_full[1], 1)

            with pe.Fori(0, DEPTH) as l:
                st = Step(l, "start")
                n = st("bank0")
                with pe.Fori(0, ADA_H) as i:
                    pe.wait_ge(aux_free[0], n + AUX_CREDIT)
                    for s in range(2):
                        pe.wait_ge(ada_step, l * (ADA * KB) + i * (2 * KB) + (s + 1) * KB)
                        for j in range(2):
                            last = mm(ab[0][:, bass.ds(i * 4 + (2 * s + j), 1)], ada_acc[:, s, j * P:(j + 1) * P],
                                      ones[:, 0:1], start=True, stop=True)
                        last.then_inc(ada_out, 1)
                pe.drain().then_inc(aux_full[0], 1)
                norm(st)

                b = aux(st, 2)
                pe.wait_ge(S_["dtw"], st.at("dtw", 1) + 1)
                for k in range(KB):
                    pe.wait_ge(S_["h_lo"], st.at("h_lo", k) + 1)
                    mm(b[:], dtw_hi[:, k, :], h_hi[:, k, :], start=k == 0, stop=False)
                    mm(b[:], dtw_hi[:, k, :], h_lo[:, k, :], start=False, stop=False)
                    last = mm(b[:], dtw_lo[:, k, :], h_hi[:, k, :], start=False, stop=k == KB - 1)
                last.then_inc(aux_full[2], 1)

                def dt_to_tokens():
                    b = aux(st, 3)
                    pe.wait_ge(S_["dt_v"], st("dt_v") + 1)
                    for t in range(TB):
                        last = nc.tensor.transpose(b[:, t * P:t * P + 3 * HEADS], dt_rows[:, t * P:(t + 1) * P],
                                                   ident[0:3 * HEADS, 0:3 * HEADS])
                    last.then_inc(aux_full[3], 1)
                    st.end()

                with pe.Fori(0, N_BC // 2) as i:
                    for slot in range(2):
                        unit(l, i + U_BC // 2, slot, h_hi, h_lo)

                def turn_xs(i, s):
                    step = Step(l, "xs", i)
                    for j in range(2):
                        pe.wait_ge(S_["silu"], step.at("silu", 2 * s + j) + (1 + SILU_CREDIT))
                        pe.wait_ge(aux_free[j], step.at(f"bank{j}", s) + AUX_CREDIT)
                        transposes(ab[j], lambda t: xsf[:, 2 * s + j, t * P:(t + 1) * P]).then_inc(aux_full[j], 1)

                def xs_round(i, first):
                    unit(l, i + U_XS // 2, 0, h_hi, h_lo)
                    if not first:
                        turn_xs(i - 1, 1)
                    unit(l, i + U_XS // 2, 1, h_hi, h_lo)
                    turn_xs(i, 0)

                xs_round(0, True)
                dt_to_tokens()
                with pe.Fori(1, N_XS // 2) as i:
                    xs_round(i, False)
                turn_xs(N_XS // 2 - 1, 1)

                with pe.Fori(0, GROUPS) as g:
                    st = Step(l, "ssd", g)

                    def spread(r):
                        b = aux(st, 2 + r % 2)
                        mm(b[:], selg[:, r:r + 1].broadcast_to([2 * HEADS, P]), acum[:], start=True, stop=True)\
                            .then_inc(aux_full[2 + r % 2], 1)

                    def diagonal(r, b):
                        pe.wait_ge(S_["m"], st("m") + 1)
                        for t in range(TB):
                            last = mm(b[:, t * P + (r % 2) * HD:t * P + (r % 2 + 1) * HD], decayed[:, r % 2, t, :],
                                      xdt[:, t, r * HD:(r + 1) * HD], start=True, stop=True)
                        last.then_inc(S_["m_used"], 1)
                        st("m_used")

                    def chunk_state(t):
                        b = aux(st, 0)
                        pe.wait_ge(S_["xd"], st("xd") + 1)
                        if t == 0:
                            pe.wait_ge(S_["b_tok"], st("b_tok") + 1)
                        mm(b[:], b_tok[:, t, :], xd[:, t, :], start=True, stop=True).then_inc(aux_full[0], 1)

                    def off_diagonal(t):
                        b = aux(st, 0)
                        pe.wait_ge(S_["state"], st("state") + 1)
                        mm(b[:], cg[:, t * P:(t + 1) * P], state[:, (t - 1) % 2, :], start=True, stop=True)\
                            .then_inc(aux_full[0], 1)

                    pe.wait_ge(S_["bc_copy"], st("bc_copy") + 1)
                    b = aux(st, 0)
                    for r in range(HG):
                        last = mm(b[:, r * TB:(r + 1) * TB], selg[:, r:r + 1].broadcast_to([2 * HEADS, P]),
                                  acum[:, P - 1:S:P], start=True, stop=True)
                    last.then_inc(aux_full[0], 1)
                    b = aux(st, 0)
                    for t in range(TB):
                        last = mm(b[:, t * P:(t + 1) * P], bg[:, t * P:(t + 1) * P], cg[:, t * P:(t + 1) * P],
                                  start=True, stop=True)
                    last.then_inc(aux_full[0], 1)
                    b = aux(st, 1)
                    transposes(b, lambda t: bg[:, t * P:(t + 1) * P]).then_inc(aux_full[1], 1)
                    spread(0)
                    spread(1)
                    unit(l, g + U_GATE // 2, 0, h_hi, h_lo)
                    between = {0: (chunk_state, 0), 1: (off_diagonal, 1), 2: (chunk_state, 1),
                               3: (off_diagonal, 2), 4: (chunk_state, 2), 6: (off_diagonal, 3)}
                    for r in range(HG):
                        if r % 2 == 0:
                            b = aux(st, 1)
                        diagonal(r, b)
                        if r % 2:
                            pe.drain().then_inc(aux_full[1], 1)
                        if r + 2 < HG:
                            spread(r + 2)
                        if r in between:
                            step, t = between[r]
                            step(t)
                    unit(l, g + U_GATE // 2, 1, h_hi, h_lo)
                    st.end()

                with pe.Fori(0, 2) as i:
                    st = Step(l, "z", i)
                    for u in range(4):
                        unit_tok(l, i * 4 + (U_ZS // 2 + u // 2), u % 2)

                    for gg in range(2):
                        for q in range(4):
                            b = aux(st, q % 2)
                            pe.wait_ge(S_["yn"], st("yn") + 1)
                            transposes(b, lambda t: yn[:, t, :]).then_inc(aux_full[q % 2], 1)
                    for u in range(4):
                        def y_ready(k):
                            if u == 0:
                                pe.wait_ge(S_["y_lo"], st("y_lo") + 1)
                        unit(l, i * 4 + (U_ZS // 2 + 2 + u // 2), u % 2, op_hi, op_lo, y_ready)
                    st.end()

                with pe.Fori(0, 2) as i:
                    st = Step(l, "att", i)
                    for pair in range(2):
                        for u in range(3):
                            n = 3 * pair + u
                            if u < 2:
                                unit(l, i * 3 + (U_QKV // 2 + n // 2), n % 2, h_hi, h_lo)
                            else:
                                unit_tok(l, i * 3 + (U_QKV // 2 + n // 2), n % 2)

                        def scores(h, j):
                            for part in range(2):
                                rows = slice(part * AD, (part + 1) * AD)
                                b = aux(st, part)
                                mm(b[:, 0:(j + 1) * P], qT[rows, h, j * P:(j + 1) * P], kT[rows, h, 0:(j + 1) * P],
                                   start=True, stop=True).then_inc(aux_full[part], 1)

                        def weigh(h, j, b):
                            pe.wait_ge(S_["pt"], st("pt") + 1)
                            for t in range(j + 1):
                                last = mm(b[:, j * P:(j + 1) * P], probsT[:, j % 2, t * P:(t + 1) * P],
                                          v_tok[:, t, h * P:(h + 1) * P], start=t == 0, stop=t == j)
                            if j == TB - 1:
                                last.then_inc(aux_full[3], 1)

                        def turn_probs(h, j):
                            b = aux(st, 2)
                            pe.wait_ge(S_["p"], st("p") + 1)
                            transposes(b, lambda t: probs[:, j % 2, 0, t * P:(t + 1) * P], n=j + 1)\
                                .then_inc(aux_full[2], 1)

                        def turn_o():
                            b = aux(st, 2)
                            pe.wait_ge(S_["on"], st("on") + 1)
                            transposes(b, lambda t: o_n[:, t, :]).then_inc(aux_full[2], 1)

                        pe.wait_ge(S_["rope"], st.at("rope", 4 * pair + 3) + (1 + ROPE_CREDIT))
                        pe.wait_ge(S_["v"], st.at("v", pair) + 1)
                        steps = [(h, j) for h in range(2) for j in range(TB)]
                        scores(*steps[0])
                        for n, (h, j) in enumerate(steps):
                            if n + 1 < len(steps):
                                scores(*steps[n + 1])
                            turn_probs(h, j)
                            if n:
                                hh, jj = steps[n - 1]
                                if jj == 0:
                                    b3 = aux(st, 3)
                                weigh(hh, jj, b3)
                            if n == TB + 1:
                                turn_o()
                        weigh(1, TB - 1, b3)
                        turn_o()
                    st.end()

                st = Step(l, "mix")
                pe.wait_ge(S_["o_lo"], PHASES_AT(l, "att", "o_lo", 8))
                for u in range(N_AO):
                    unit(l, U_AO // 2 + u // 2, u % 2, op_hi, op_lo)
                for u in range(N_WO):
                    def mixed(k):
                        if u == 0:
                            pe.wait_ge(S_["mix_lo"], st("mix_lo") + 1)
                    unit(l, U_WO // 2 + u // 2, u % 2, h_hi, h_lo, mixed)
                norm(st)
                with pe.Fori(0, 4) as i:
                    sf = Step(l, "ff", i)
                    for u in range(4):
                        def normed(k):
                            pe.wait_ge(S_["h_lo"], st.at("h_lo", k) + 1)
                        unit(l, i * 4 + (U_FF // 2 + u // 2), u % 2, h_hi, h_lo, normed if u == 0 else None)
                    for u in range(4):
                        def squared(k):
                            if u == 0:
                                pe.wait_ge(S_["u_lo"], sf("u_lo") + (1 + U_CREDIT))
                        unit(l, i * 4 + (U_FF // 2 + 2 + u // 2), u % 2, op_hi, op_lo, squared)
                    sf.end()
                st.end()
            norm(Step(DEPTH, "start"))

        def act_program(act):
            A = nc.scalar.activation

            def convert(l, nh, slot):
                wait(act, raw_in[slot], raw_at(l, nh + ADA_H))
                wait(act, gemm_done, (l * UNITS + nh * 2) * 2 + (2 * slot + 2))
                A(w_hi[:, slot], raw[:, slot], ACT.Copy).then_inc(hi_ready, 1)

            def full(step, b):
                wait(act, aux_full[b], step(f"bank{b}") + 1)
                return ab[b]

            def norm(step, src, shift):
                for k in range(KB):
                    n = step("sq")
                    if k >= 2:
                        wait(act, S_["sq_used"], step.at("sq_used", k - 2) + 1)
                    A(sq[:, k % 2], src[:, k], ACT.Square).then_inc(S_["sq"], 1)
                for k in range(KB):
                    wait(act, S_["pre"], step("pre") + 1)
                    if shift is not None:
                        A(h_hi[:, k], pre[:, k % 2], ACT.Identity, bias=shift(k)).then_inc(S_["h_hi"], 1)
                        step("h_hi")

            act.wait_ge(con_in, 16)
            A(cact[:, KB:2 * KB], con[:, K_C:K_C + KB], ACT.Tanh, scale=0.5).then_inc(c_tanh, 1)
            act.wait_ge(x_in, 16)
            with act.Fori(0, DEPTH) as l:
                st = Step(l, "start")
                wait(act, S_["lam"], st("lam") + 1)
                A(lams[:, 2:4], lams[:, 0:2], ACT.Exp)
                A(a_neg[0:HEADS, 0:1], par[0:HEADS, C_ALOG:C_ALOG + 1], ACT.Exp).then_inc(S_["lam"], 1)
                wait(act, dtw_in, (l + 1) * 16)
                A(dtw_hi[:], dtw_raw[:], ACT.Copy).then_inc(S_["dtw"], 1)
                st("lam"), st("dtw"), st("dtw")
                wait(act, S_["layer"], l + LAYER_CREDIT)

                def first_norm_part():
                    for k in range(KB):
                        if k >= 2:
                            wait(act, S_["sq_used"], st.at("sq_used", k - 2) + 1)
                        A(sq[:, k % 2], x[:, k], ACT.Square).then_inc(S_["sq"], 1)
                first_norm_part()
                for k in range(KB):
                    wait(act, S_["pre"], st("pre") + 1)
                    A(h_hi[:, k], pre[:, k % 2], ACT.Identity, bias=ada_v[:, 0, k:k + 1]).then_inc(S_["h_hi"], 1)
                convert(l, 0, 0)
                convert(l, 0, 1)
                b = ab[2]
                wait(act, aux_full[2], st.at("bank2", 0) + 1)
                A(dt_x[:], b[0:HEADS, :], ACT.Identity, bias=par[0:HEADS, C_DTB:C_DTB + 1]).then_inc(aux_free[2], 1)
                act.drain()
                A(dt_e[:], dt_x[:], ACT.Abs)
                act.drain()
                A(dt_e[:], dt_e[:], ACT.Exp, scale=-1.0).then_inc(S_["dt_a"], 1)

                def conv_seed(step, nh, slot, j, block):
                    c = 2 * slot + j
                    wait(act, gemm_done, done_at(l, nh * 2 + slot, j))
                    wait(act, S_["silu"], step.at("silu", c - 4) + (1 + SILU_CREDIT))
                    A(conv[:, c], gb[c][:], ACT.Identity, scale=cw[:, bass.ds(block * CONV + (CONV - 1), 1)],
                      bias=cw[:, bass.ds(block + CONV * CONV_BLOCKS, 1)]).then_inc(S_["seed"], 1)
                    step("seed")

                def conv_tanh(step, c):
                    wait(act, S_["taps"], step("taps") + 1)
                    A(ctanh[:, c], conv[:, c], ACT.Tanh).then_inc(S_["tanh"], 1)
                    step("tanh")

                with act.Fori(0, N_BC // 2) as i:
                    step = Step(l, "bc", i)
                    for slot in range(2):
                        convert(l, i + 1, slot)
                        for j in range(2):
                            conv_seed(step, i + U_BC // 2, slot, j, i * 4 + (2 * slot + j))
                        for j in range(2):
                            conv_tanh(step, 2 * slot + j)
                    step.end()

                def x_to_tok(i, s):
                    step = Step(l, "xs", i)
                    for j in range(2):
                        wait(act, aux_full[j], step.at(f"bank{j}", s) + 1)
                        A(y_tok[:, :, bass.ds(i * (4 * P) + (2 * s + j) * P, P)],
                          ab[j][:].rearrange("p (t n) -> p t n", t=TB), ACT.Copy).then_inc(aux_free[j], 1)

                def xs_round(i, first):
                    step = Step(l, "xs", i)
                    for slot in range(2):
                        convert(l, i + (U_XS // 2 + 1), slot)
                        for j in range(2):
                            conv_seed(step, i + U_XS // 2, slot, j, i * 4 + (2 * N_BC + 2 * slot + j))
                        for j in range(2):
                            conv_tanh(step, 2 * slot + j)
                        if slot == 0 and not first:
                            x_to_tok(i - 1, 1)
                        if slot == 1:
                            x_to_tok(i, 0)

                wait(act, x_saved, (l + 1) * 16)
                xs_round(0, True)
                wait(act, aux_full[3], st.at("bank3", 0) + 1)
                A(tok[:], ab[3][:].rearrange("p (t n) -> p t n", t=TB)[:, :, 0:3 * HEADS], ACT.Copy)\
                    .then_inc(aux_free[3], 1)
                act.drain()
                A(ea_tok[:], tok[:, :, HEADS:2 * HEADS], ACT.Exp, scale=-1.0)
                A(dec_tok[:], tok[:, :, 2 * HEADS:3 * HEADS], ACT.Exp).then_inc(S_["dt_a"], 1)
                with act.Fori(1, N_XS // 2) as i:
                    xs_round(i, False)
                x_to_tok(N_XS // 2 - 1, 1)
                act.drain().then_inc(S_["x_tok"], 1)

                with act.Fori(0, GROUPS) as g:
                    st = Step(l, "ssd", g)
                    wait(act, S_["y"], l * TOTAL["y"] + g + 1)
                    A(bg[:], bct[:, bass.ds(g, 1), :].rearrange("p a n -> p (a n)"), ACT.Copy)
                    A(cg[:], bct[:, bass.ds(g + GROUPS, 1), :].rearrange("p a n -> p (a n)"), ACT.Copy)
                    A(selg[:], con[0:2 * HEADS, bass.ds(g * HG + K_SEL, HG)], ACT.Copy).then_inc(S_["bc_copy"], 1)
                    st("bc_copy")
                    b = full(st, 0)
                    A(cdec[:].rearrange("p h t -> p (h t)"), b[:, 0:HG * TB], ACT.Exp).then_inc(aux_free[0], 1)
                    act.drain().then_inc(S_["cdec"], 1)
                    b = full(st, 1)
                    A(b_tok[:], b[:].rearrange("p (t n) -> p t n", t=TB), ACT.Copy).then_inc(aux_free[1], 1)
                    act.drain().then_inc(S_["b_tok"], 1)

                    def decay(r):
                        wait(act, S_["sum"], st("sum") + 1)
                        tile = seg[:, r % 2].rearrange("p t n -> p (t n)")
                        A(tile, tile, ACT.Relu, scale=-1.0)
                        act.drain()
                        A(tile, tile, ACT.Exp, scale=-1.0).then_inc(S_["seg"], 1)
                        st("seg")

                    def gate(slot):
                        for j in range(2):
                            wait(act, gemm_done, done_at(l, (g + U_GATE // 2) * 2 + slot, j))
                            dst = gates[:, bass.ds(g * 4 + (2 * slot + j), 1), :].rearrange("p a n -> p (a n)")
                            A(dst, gb[2 * slot + j][:], ACT.Tanh, scale=0.5).then_inc(bank_free[slot], 1)

                    decay(0)
                    decay(1)
                    convert(l, g + (U_GATE // 2 + 1), 0)
                    gate(0)
                    for r in range(2, HG):
                        decay(r)
                    convert(l, g + (U_GATE // 2 + 1), 1)
                    gate(1)

                with act.Fori(0, 2) as i:
                    st = Step(l, "z", i)
                    base = U_ZS // 2
                    for gg in range(2):
                        for slot in range(2):
                            convert(l, i * 4 + (base + gg + 1), slot)
                            for j in range(2):
                                wait(act, gemm_done, done_at(l, (i * 4 + (base + gg)) * 2 + slot, j))
                                st("z_act")
                                wait(act, S_["z_used"], st.at("z_used", 4 * gg + 2 * slot + j) + Z_CREDIT)
                                src = gb[2 * slot + j][:].rearrange("p (t n) -> p t n", t=2)
                                A(zt[:], src, ACT.Tanh, scale=0.5)
                                A(zh[:], src, ACT.Copy, scale=0.5).then_inc(bank_free[slot], 1)
                                act.drain().then_inc(S_["z_act"], 1)
                        wait(act, S_["y_gate"], st("y_gate") + 1)
                        for t in range(TB):
                            last = A(yn[:].rearrange("p t n -> p (t n)"), y_tok[:, t, bass.ds(i * (2 * GW) + gg * GW, GW)],
                                     ACT.Square, accum_out=y_ms[:, t:t + 1])
                            act.drain()
                        act.drain().then_inc(S_["y_sq"], 1)
                        for q in range(4):
                            b = full(st, q % 2)
                            A(op_hi[:, 4 * gg + q, :], b[:], ACT.Copy,
                              scale=par[:, bass.ds(i * 8 + (C_SNG + 4 * gg + q), 1)]).then_inc(S_["y_hi"], 1)
                            st("y_hi")
                    for u in range(4):
                        convert(l, i * 4 + (base + 3 + u // 2), u % 2)

                with act.Fori(0, 2) as i:
                    st = Step(l, "att", i)
                    base = U_QKV // 2
                    for pair in range(2):
                        for u in range(2):
                            n = 3 * pair + u
                            convert(l, i * 3 + (base + n // 2 + 1), n % 2)
                            for j in range(2):
                                c = 2 * (n % 2) + j
                                wait(act, gemm_done, done_at(l, i * 6 + (U_QKV + n), j))
                                wait(act, S_["rope"], st("rope") + 1)
                                for quarter in range(4):
                                    src = quarter ^ 1
                                    last = A(swap[quarter * 32:quarter * 32 + 32, :], gb[c][src * 32:src * 32 + 32, :],
                                             ACT.Copy)
                                last.then_inc(S_["swap"], 1)
                                st("swap")
                        n = 3 * pair + 2
                        convert(l, i * 3 + (base + n // 2 + 1), n % 2)
                        for j in range(2):
                            wait(act, gemm_done, done_at(l, i * 6 + (U_QKV + n), j))
                            A(v_tok[:, 2 * j:2 * j + 2, :], gb[2 * (n % 2) + j][:].rearrange("p (t n) -> p t n", t=2),
                              ACT.Copy).then_inc(bank_free[n % 2], 1)
                        act.drain().then_inc(S_["v"], 1)
                        st("v")

                        def expo(h, j):
                            wait(act, S_["mx"], st("mx") + 1)
                            for part in range(2):
                                b = ab[part]
                                last = A(probs[:, j % 2, part, 0:(j + 1) * P], b[:, 0:(j + 1) * P], ACT.Exp,
                                         scale=AD ** -0.5, bias=mxn[:, 2 * (j % 2) + part:2 * (j % 2) + part + 1],
                                         accum_out=den[:, 2 * (j % 2) + part:2 * (j % 2) + part + 1])
                                act.drain().then_inc(aux_free[part], 1)
                            act.drain().then_inc(S_["e"], 1)
                            st("e")

                        def probs_out(h, j):
                            b = full(st, 2)
                            A(probsT[:, j % 2, 0:(j + 1) * P], b[:, 0:(j + 1) * P], ACT.Copy).then_inc(aux_free[2], 1)
                            act.drain().then_inc(S_["pt"], 1)
                            st("pt")

                        def o_square():
                            b = full(st, 3)
                            for t in range(TB):
                                A(o_n[:, t, :], b[:, t * P:(t + 1) * P], ACT.Square, accum_out=y_ms[:, t:t + 1])
                            act.drain().then_inc(S_["o_sq"], 1)
                            st("o_sq")

                        def o_out(h):
                            b = full(st, 2)
                            A(op_hi[:, bass.ds(i * 4 + (2 * pair + h), 1), :].rearrange("p a n -> p (a n)"), b[:],
                              ACT.Copy, scale=subg[:, 0:1]).then_inc(S_["o_hi"], 1)
                            st("o_hi")

                        steps = [(h, j) for h in range(2) for j in range(TB)]
                        expo(*steps[0])
                        for n, (h, j) in enumerate(steps):
                            if n + 1 < len(steps):
                                expo(*steps[n + 1])
                            probs_out(h, j)
                            if n == TB:
                                o_square()
                            if n == TB + 1:
                                o_out(0)
                        o_square()
                        o_out(1)

                st = Step(l, "mix")
                for u in range(N_AO):
                    convert(l, U_AO // 2 + 1 + u // 2, u % 2)
                for k in range(KB):
                    if k == 0:
                        wait(act, S_["mixed"], st("mixed") + 1)
                    A(h_hi[:, k], mix[:, k], ACT.Copy).then_inc(S_["mix_hi"], 1)
                for u in range(N_WO):
                    convert(l, U_WO // 2 + 1 + u // 2, u % 2)
                wait(act, S_["x_sum"], st("x_sum") + 1)
                norm(st, x, lambda k: ada_v[:, 3, k:k + 1])

                def ff_round(i, last_round):
                    sf = Step(l, "ff", i)
                    for u in range(8):
                        if u < 6 or not last_round:
                            convert(l, i * 4 + (U_FF // 2 + u // 2 + 1), u % 2)
                        if u < 4:
                            for j in range(2):
                                wait(act, gemm_done, done_at(l, i * 8 + (U_FF + u), j))
                                c = 2 * (u % 2) + j
                                wait(act, S_["u_lo"], sf.at("u_lo", 2 * u + j - 4) + (1 + U_CREDIT))
                                A(relu[:, c], gb[c][:], ACT.Relu).then_inc(bank_free[u % 2], 1)
                                act.drain().then_inc(S_["relu"], 1)
                                A(op_hi[:, 2 * u + j, :], relu[:, c], ACT.Square).then_inc(S_["u_hi"], 1)
                with act.Fori(0, 3) as i:
                    ff_round(i, False)
                ff_round(3, True)
            wait(act, S_["layer"], DEPTH + LAYER_CREDIT)
            norm(Step(DEPTH, "start"), x, None)

        def dve_program(dve):
            v = nc.vector
            TT, TS, STT = v.tensor_tensor, v.tensor_scalar, v.scalar_tensor_tensor

            def full(step, b):
                wait(dve, aux_full[b], step(f"bank{b}") + 1)
                return ab[b]

            def settle():
                dve.drain()

            v.memset(ones[:], 1.0)
            v.memset(half[:], -0.5)
            settle()
            dve.drain().then_inc(ready, 1)
            dve.sem_inc(S_["layer"], LAYER_CREDIT)
            for b in range(4):
                dve.sem_inc(aux_free[b], AUX_CREDIT)
            for s in range(2):
                dve.sem_inc(bank_free[s], BANK_CREDIT)
            dve.sem_inc(S_["y"], Y_CREDIT)
            dve.sem_inc(S_["silu"], SILU_CREDIT)
            dve.sem_inc(S_["z_used"], Z_CREDIT)
            dve.sem_inc(S_["u_lo"], U_CREDIT)
            dve.sem_inc(S_["rope"], ROPE_CREDIT)
            dve.wait_ge(c_tanh, 1)
            TS(cact[:, 0:KB], con[:, K_C:K_C + KB], 0.5, None, ALU.mult)
            settle()
            STT(cact[:, 0:KB], cact[:, KB:2 * KB], 1.0, cact[:, 0:KB], ALU.add, ALU.mult)
            settle()

            def norm(step, mul, shift):
                for k in range(KB):
                    wait(dve, S_["sq"], step("sq") + 1)
                    if k == 0:
                        v.tensor_copy(ss[:], sq[:, 0]).then_inc(S_["sq_used"], 1)
                    else:
                        TT(ss[:], ss[:], sq[:, k % 2], ALU.add).then_inc(S_["sq_used"], 1)
                    settle()
                    step("sq_used")
                dve.drain().then_inc(S_["ss"], 1)
                b = full(step, 0)
                TS(ms[:], b[:, 0:TB], 1.0 / D, EPS, ALU.mult, ALU.add).then_inc(aux_free[0], 1)
                dve.drain().then_inc(S_["ms"], 1)
                b = full(step, 1)
                for k in range(KB + 1):
                    if k < KB:
                        if shift is not None and k >= 2:
                            wait(dve, S_["h_hi"], step.at("h_hi", k - 2) + 1)
                        dst = pre[:, k % 2] if shift is not None else y_out[:, k]
                        STT(dst, x[:, k], mul(k), b[:], ALU.mult, ALU.mult).then_inc(S_["pre"], 1)
                        if k == KB - 1:
                            dve.drain().then_inc(aux_free[1], 1)
                    if k and shift is not None:
                        wait(dve, S_["h_hi"], step("h_hi") + 1)
                        STT(h_lo[:, k - 1], pre[:, (k - 1) % 2], shift(k - 1), h_hi[:, k - 1].bitcast(F32), ALU.add,
                            ALU.subtract).then_inc(S_["h_lo"], 1)
                        settle()

            with dve.Fori(0, DEPTH) as l:
                st = Step(l, "start")
                wait(dve, par_in, (l + 1) * 16)
                lv = par[:, C_LAM:C_LAM + 4 * AD].rearrange("p (a b n) -> p a b n", a=2, b=2)
                TT(lamw[:].rearrange("p (a n) -> p a n", a=2), lv[:, :, 0, :], lv[:, :, 1, :], ALU.mult)
                settle()
                v.tensor_reduce(lams[:, 0:2], lamw[:].rearrange("p (a n) -> p a n", a=2), AX_X, ALU.add)\
                    .then_inc(S_["lam"], 1)
                TS(cw[:], par[:, C_CW:C_CW + (CONV + 1) * CONV_BLOCKS], 0.5, None, ALU.mult)
                TT(subg[:], par[:, C_SUB:C_SUB + 1], par[:, C_OML:C_OML + 1], ALU.mult)
                wait(dve, S_["lam"], st.at("lam", 1) + 1)
                TT(lams[:, 1:2], lams[:, 3:4], lams[:, 2:3], ALU.subtract)
                TS(a_neg[0:HEADS, 1:2], a_neg[0:HEADS, 0:1], -1.0, None, ALU.mult)
                settle()
                TT(lams[:, 0:1], lams[:, 1:2], par[:, C_LI:C_LI + 1], ALU.subtract)
                wait(dve, S_["dtw"], st.at("dtw", 0) + 1)
                TT(dtw_lo[:], dtw_raw[:], dtw_hi[:].bitcast(F32), ALU.subtract).then_inc(S_["dtw"], 1)

                with dve.Fori(0, ADA_H) as i:
                    for s in range(2):
                        wait(dve, raw_in[s], raw_at(l, i))
                        for k in range(KB):
                            if k == 0:
                                wait(dve, ada_out, l * ADA + i * 2 + (s + 1))
                                TS(ada_acc[:, s], raw[:, s, 0], cact[:, 0:1], None, ALU.mult).then_inc(ada_step, 1)
                            else:
                                wait(dve, ada_step, l * (ADA * KB) + i * (2 * KB) + (s * KB + k))
                                STT(ada_acc[:, s], raw[:, s, k], cact[:, k:k + 1], ada_acc[:, s], ALU.mult, ALU.add)\
                                    .then_inc(ada_step, 1)
                b = full(st, 0)
                TT(ada[:], b[:, 0:6 * KB], par[:, C_BADA:C_BADA + 6 * KB], ALU.add).then_inc(aux_free[0], 1)
                settle()
                for m, (scale_at, norm_at) in enumerate(((1, C_N1), (4, C_N2))):
                    STT(amul[:, m * KB:(m + 1) * KB], ada_v[:, scale_at, :], 1.0, par[:, norm_at:norm_at + KB],
                        ALU.add, ALU.mult)
                TS(g1h[:], ada_v[:, 2, :], 0.5, None, ALU.mult)
                settle()
                norm(st, lambda k: amul[:, k:k + 1], lambda k: ada_v[:, 0, k:k + 1])

                v.memset(dt_one[:], 1.0)
                wait(dve, S_["dt_a"], st.at("dt_a", 0) + 1)
                TS(dt_s[:], dt_e[:], 2.0, None, ALU.add)
                settle()
                v.reciprocal(dt_s2[:], dt_s[:])
                settle()
                TT(dt_s[:], dt_e[:], dt_s2[:], ALU.mult)
                settle()
                TT(dt_s2[:], dt_s[:], dt_s[:], ALU.mult)
                settle()
                TS(dt_p[:], dt_s2[:], 1.0 / 17, None, ALU.mult)
                for odd in (15, 13, 11, 9, 7, 5, 3):
                    settle()
                    STT(dt_p[:], dt_p[:], 1.0 / odd, dt_s2[:], ALU.add, ALU.mult)
                settle()
                STT(dt_p[:], dt_p[:], 1.0, dt_s[:], ALU.add, ALU.mult)
                TS(dt_x[:], dt_x[:], 0.0, None, ALU.max)
                settle()
                STT(dt_rows[0:HEADS], dt_p[:], 2.0, dt_x[:], ALU.mult, ALU.add)
                settle()
                TS(dt_s[:], dt_rows[0:HEADS], a_neg[0:HEADS, 1:2], None, ALU.mult)
                settle()
                for t in range(TB):
                    c = slice(t * P, (t + 1) * P)
                    v.tensor_tensor_scan(dt_cum[:, c], dt_one[:, c], dt_s[:, c], 0.0, ALU.mult, ALU.add)
                settle()
                v.tensor_copy(acum[0:HEADS], dt_cum[:])
                TS(dt_rows[HEADS:2 * HEADS], dt_cum[:], -1.0, None, ALU.mult)
                for t in range(TB):
                    c = slice(t * P, (t + 1) * P)
                    TS(dt_rows[2 * HEADS:3 * HEADS, c], dt_cum[:, c], -1.0, dt_cum[:, (t + 1) * P - 1:(t + 1) * P],
                       ALU.mult, ALU.add)
                settle()
                TT(acum[HEADS:2 * HEADS], dt_cum[:], acum[0:HEADS].bitcast(F32), ALU.subtract)
                dve.drain().then_inc(S_["dt_v"], 1)

                def taps(step, nh, slot, j, block):
                    c = 2 * slot + j
                    wait(dve, S_["seed"], step("seed") + 1)
                    for lag in range(1, CONV):
                        last = STT(conv[:, c, lag:S], gb[c][:, 0:S - lag],
                                   cw[:, bass.ds(block * CONV + (CONV - 1 - lag), 1)], conv[:, c, lag:S], ALU.mult, ALU.add)
                        if lag == CONV - 1:
                            last.then_inc(bank_free[slot], 1)
                        else:
                            settle()
                    dve.drain().then_inc(S_["taps"], 1)

                def silu(step, c, dst):
                    wait(dve, S_["tanh"], step("tanh") + 1)
                    STT(dst, ctanh[:, c], 1.0, conv[:, c], ALU.add, ALU.mult).then_inc(S_["silu"], 1)

                def conv_round(step, base, block, dst):
                    for c in range(4):
                        taps(step, base, c // 2, c % 2, block + c)
                        if c:
                            silu(step, c - 1, dst(c - 1))
                    silu(step, 3, dst(3))

                with dve.Fori(0, N_BC // 2) as i:
                    conv_round(Step(l, "bc", i), i + U_BC // 2, i * 4,
                               lambda c: bct[:, bass.ds(i * 4 + c, 1), :].rearrange("p a n -> p (a n)"))

                def xs_dst(c, i):
                    return xsf[:, c]

                def xs_round(i, first):
                    step = Step(l, "xs", i)
                    for c in range(4):
                        taps(step, i, c // 2, c % 2, i * 4 + (2 * N_BC + c))
                        for d in ([c - 1] if c else []) + ([3] if c == 3 else []):
                            if not first:
                                wait(dve, aux_full[d % 2], step.at(f"bank{d % 2}", d // 2 - 2) + 1)
                            silu(step, d, xsf[:, d])

                xs_round(0, True)
                with dve.Fori(1, N_XS // 2) as i:
                    xs_round(i, False)

                with dve.Fori(0, GROUPS) as g:
                    st = Step(l, "ssd", g)
                    yv = y_tok[:, :, bass.ds(g * GW, GW)]

                    def seg_sum(r):
                        b = full(st, 2 + r % 2)
                        TT(seg[:, r % 2], b[:].rearrange("p (t n) -> p t n", t=TB),
                           tok[:, :, bass.ds(g * HG + (HEADS + r), 1)].broadcast_to([P, TB, P]), ALU.add)\
                            .then_inc(aux_free[2 + r % 2], 1)
                        dve.drain().then_inc(S_["sum"], 1)

                    def masked(r):
                        wait(dve, S_["seg"], st("seg") + 1)
                        if r >= 2:
                            wait(dve, S_["m_used"], st.at("m_used", r - 2) + 1)
                        TT(decayed[:, r % 2], seg[:, r % 2], cbm[:], ALU.mult).then_inc(S_["m"], 1)

                    seg_sum(0)
                    seg_sum(1)
                    st("bank0")
                    b = full(st, 0)
                    TT(cbm[:], b[:].rearrange("p (t n) -> p t n", t=TB),
                       con[:, K_TRI:K_TRI + P].unsqueeze(1).broadcast_to([P, TB, P]), ALU.mult).then_inc(aux_free[0], 1)
                    settle()
                    st("bank1")

                    def y_diag(r):
                        b = full(st, 1)
                        dst = yv[:, :, (r - 1) * HD:(r + 1) * HD]
                        TT(dst, dst, b[:].rearrange("p (t n) -> p t n", t=TB), ALU.add).then_inc(aux_free[1], 1)

                    def heads(ap):
                        return ap.rearrange("p (h n) -> p h n", h=HG)

                    def next_state(t):
                        b = full(st, 0)
                        if t == 0:
                            v.tensor_copy(state[:, 0], b[:]).then_inc(aux_free[0], 1)
                        else:
                            TT(heads(state[:, t % 2]), heads(state[:, (t - 1) % 2]),
                               cdec[:, :, t:t + 1].broadcast_to([P, HG, HD]), ALU.mult)
                            settle()
                            TT(state[:, t % 2], state[:, t % 2], b[:], ALU.add).then_inc(aux_free[0], 1)
                        dve.drain().then_inc(S_["state"], 1)

                    def y_offset(t):
                        b = full(st, 0)
                        TT(heads(y_off[:]), heads(b[:]),
                           ea_tok[:, t, bass.ds(g * HG, HG)].unsqueeze(2).broadcast_to([P, HG, HD]), ALU.mult)\
                            .then_inc(aux_free[0], 1)
                        settle()
                        TT(yv[:, t, :], yv[:, t, :], y_off[:], ALU.add)
                        settle()

                    wait(dve, S_["xd"], st.at("xd", 2) + 1)
                    wait(dve, S_["cdec"], st("cdec") + 1)
                    between = {0: (next_state, 0), 1: (y_offset, 1), 2: (next_state, 1), 3: (y_offset, 2),
                               4: (next_state, 2), 6: (y_offset, 3)}
                    for r in range(HG):
                        masked(r)
                        if r + 2 < HG:
                            seg_sum(r + 2)
                        if r % 2:
                            y_diag(r)
                        if r in between:
                            step, t = between[r]
                            step(t)
                    dve.drain().then_inc(S_["y"], 1)

                v.memset(mix[:], 0.0)
                settle()

                def block_of(t, n):
                    return t[:, bass.ds(n, 1), :].rearrange("p a n -> p (a n)")

                with dve.Fori(0, 2) as i:
                    st = Step(l, "z", i)
                    for gg in range(2):
                        for slot in range(2):
                            for j in range(2):
                                wait(dve, S_["z_act"], st("z_act") + 1)
                                STT(zt[:], zt[:], 1.0, zh[:], ALU.add, ALU.mult)
                                settle()
                                yv = y_tok[:, 2 * j:2 * j + 2, bass.ds(i * (2 * GW) + (gg * GW + slot * UW), UW)]
                                TT(yv, yv, zt[:], ALU.mult)
                                dve.drain().then_inc(S_["z_used"], 1)
                        dve.drain().then_inc(S_["y_gate"], 1)
                        wait(dve, S_["y_sq"], st("y_sq") + 1)
                        TS(y_ms[:], y_ms[:], 1.0 / GW, EPS, ALU.mult, ALU.add).then_inc(S_["y_ms"], 1)
                        wait(dve, S_["y_rs"], st("y_rs") + 1)
                        for q in range(4):
                            if q:
                                wait(dve, aux_full[(q - 1) % 2], st.at(f"bank{(q - 1) % 2}", 2 * gg + (q - 1) // 2) + 1)
                            TT(yn[:], y_tok[:, :, bass.ds(i * (2 * GW) + (gg * GW + q * P), P)],
                               y_rs[:].unsqueeze(2).broadcast_to([P, TB, P]), ALU.mult).then_inc(S_["yn"], 1)
                            if q:
                                y_low(st, i, gg, q - 1)
                        y_low(st, i, gg, 3)
                    for u in range(4):
                        for j in range(2):
                            c = 2 * (u % 2) + j
                            wait(dve, gemm_done, done_at(l, i * 8 + (U_ZS + 4 + u), j))
                            STT(zt[:].rearrange("p a n -> p (a n)"), gate_s[:, 2 * u + j, :], 1.0, gb[c][:], ALU.add, ALU.mult)\
                                .then_inc(bank_free[u % 2], 1)
                            settle()
                            TT(mix[:, 2 * u + j, :], mix[:, 2 * u + j, :], zt[:].rearrange("p a n -> p (a n)"), ALU.add)
                            settle()
                    dve.drain().then_inc(S_["z_used"], 1)

                with dve.Fori(0, 2) as i:
                    st = Step(l, "att", i)
                    wait(dve, rope_in, (l + 1) * 32)
                    for pair in range(2):
                        for u in range(2):
                            n = 3 * pair + u
                            for j in range(2):
                                c = 2 * (n % 2) + j
                                wait(dve, S_["swap"], st("swap") + 1)
                                TT(qc[:], gb[c][:], rope_cos[:], ALU.mult).then_inc(bank_free[n % 2], 1)
                                TT(swap[:], swap[:], rope_sin[:], ALU.mult)
                                settle()
                                TT((qT, kT)[u][:, j, :], qc[:], swap[:], ALU.add)
                                dve.drain().then_inc(S_["rope"], 1)

                        def maxima(h, j):
                            for part in range(2):
                                b = full(st, part)
                                TT(b[:, j * P:(j + 1) * P], b[:, j * P:(j + 1) * P], con[:, K_NEG:K_NEG + P], ALU.add)
                            settle()
                            for part in range(2):
                                v.tensor_reduce(mxs[:, part:part + 1], ab[part][:, 0:(j + 1) * P], AX_X, ALU.max)
                            settle()
                            TS(mxn[:, 2 * (j % 2):2 * (j % 2) + 2], mxs[:, 0:2], -(AD ** -0.5), None, ALU.mult)
                            dve.drain().then_inc(S_["mx"], 1)

                        def difference(h, j):
                            wait(dve, S_["e"], st("e") + 1)
                            d = slice(2 * (j % 2), 2 * (j % 2) + 2)
                            v.reciprocal(rden[:, d], den[:, d])
                            settle()
                            w = slice(0, (j + 1) * P)
                            d0, d1 = d.start, d.start + 1
                            TT(mxs[:, 2:3], rden[:, d1:d1 + 1], lams[:, 0:1], ALU.mult)
                            TS(probs[:, j % 2, 0, w], probs[:, j % 2, 0, w], rden[:, d0:d0 + 1], None, ALU.mult)
                            settle()
                            STT(probs[:, j % 2, 0, w], probs[:, j % 2, 1, w], mxs[:, 2:3], probs[:, j % 2, 0, w],
                                ALU.mult, ALU.add)
                            dve.drain().then_inc(S_["p"], 1)

                        def o_norm():
                            wait(dve, S_["o_sq"], st("o_sq") + 1)
                            TS(y_ms[:], y_ms[:], 1.0 / P, EPS, ALU.mult, ALU.add).then_inc(S_["o_ms"], 1)
                            wait(dve, S_["o_rs"], st("o_rs") + 1)
                            TT(o_n[:], ab[3][:].rearrange("p (t n) -> p t n", t=TB),
                               y_rs[:].unsqueeze(2).broadcast_to([P, TB, P]), ALU.mult).then_inc(aux_free[3], 1)
                            dve.drain().then_inc(S_["on"], 1)

                        def o_low(h):
                            wait(dve, S_["o_hi"], st("o_hi") + 1)
                            dst = bass.ds(i * 4 + (2 * pair + h), 1)
                            STT(op_lo[:, dst, :].rearrange("p a n -> p (a n)"), ab[2][:], subg[:, 0:1],
                                op_hi[:, dst, :].rearrange("p a n -> p (a n)").bitcast(F32), ALU.mult, ALU.subtract)\
                                .then_inc(aux_free[2], 1)
                            dve.drain().then_inc(S_["o_lo"], 1)

                        steps = [(h, j) for h in range(2) for j in range(TB)]
                        maxima(*steps[0])
                        for n, (h, j) in enumerate(steps):
                            if n + 1 < len(steps):
                                maxima(*steps[n + 1])
                            difference(h, j)
                            if n == TB:
                                o_norm()
                            if n == TB + 1:
                                o_low(0)
                        o_norm()
                        o_low(1)

                st = Step(l, "mix")
                for u in range(N_AO):
                    for j in range(2):
                        c = 2 * (u % 2) + j
                        wait(dve, gemm_done, done_at(l, U_AO + u, j))
                        STT(zt[:].rearrange("p a n -> p (a n)"), gate_a[:, 2 * u + j, :], 1.0, gb[c][:], ALU.add, ALU.mult)\
                            .then_inc(bank_free[u % 2], 1)
                        settle()
                        TT(mix[:, 2 * u + j, :], mix[:, 2 * u + j, :], zt[:].rearrange("p a n -> p (a n)"), ALU.add)
                        settle()
                dve.drain().then_inc(S_["mixed"], 1)
                for k in range(KB):
                    wait(dve, S_["mix_hi"], st("mix_hi") + 1)
                    TT(h_lo[:, k], mix[:, k], h_hi[:, k].bitcast(F32), ALU.subtract).then_inc(S_["mix_lo"], 1)
                wait(dve, x_back, (l + 1) * 16)
                for u in range(N_WO):
                    for j in range(2):
                        wait(dve, gemm_done, done_at(l, U_WO + u, j))
                        STT(x[:, 2 * u + j], gb[2 * (u % 2) + j][:], g1h[:, 2 * u + j:2 * u + j + 1], x[:, 2 * u + j],
                            ALU.mult, ALU.add).then_inc(bank_free[u % 2], 1)
                dve.drain().then_inc(S_["x_sum"], 1)
                norm(st, lambda k: amul[:, KB + k:KB + k + 1], lambda k: ada_v[:, 3, k:k + 1])

                with dve.Fori(0, 4) as i:
                    sf = Step(l, "ff", i)
                    for u in range(4):
                        for j in range(2):
                            c = 2 * (u % 2) + j
                            wait(dve, S_["relu"], sf("relu") + 1)
                            TT(usq[:, j], relu[:, c], relu[:, c], ALU.mult)
                            settle()
                            wait(dve, S_["u_hi"], sf("u_hi") + 1)
                            TT(op_lo[:, 2 * u + j, :], usq[:, j], op_hi[:, 2 * u + j, :].bitcast(F32), ALU.subtract)\
                                .then_inc(S_["u_lo"], 1)
                            settle()
                    for u in range(4):
                        for j in range(2):
                            wait(dve, gemm_done, done_at(l, i * 8 + (U_FF + 4 + u), j))
                            STT(x[:, 2 * u + j], gb[2 * (u % 2) + j][:], ada_v[:, 5, 2 * u + j:2 * u + j + 1],
                                x[:, 2 * u + j], ALU.mult, ALU.add).then_inc(bank_free[u % 2], 1)
                    settle()
                dve.drain().then_inc(S_["layer"], 1)
            norm(Step(DEPTH, "start"), lambda k: con[:, K_FG + k:K_FG + k + 1], None)

        def pool_program(pool):
            gp = nc.gpsimd

            def rsqrt(src, dst, step, want, give):
                wait(pool, S_[want], step(want) + 1)
                gp.tensor_tensor(dst[:], src[:], half[:], ALU.pow).then_inc(S_[give], 1)

            def low(l, nh, slot):
                wait(pool, hi_ready, l * UNITS + nh * 2 + (slot + 1))
                gp.tensor_tensor(w_lo[:, slot], raw[:, slot], w_hi[:, slot].bitcast(F32), ALU.subtract)\
                    .then_inc(lo_ready, 1)

            pool.sem_inc(lo_ready, LO_CREDIT)
            pool.sem_inc(ada_out, 2)
            pool.wait_ge(ready, 1)
            with pool.Fori(0, DEPTH) as l:
                st = Step(l, "start")
                rsqrt(ms, rs, st, "ms", "rs")
                low(l, 0, 0)
                low(l, 0, 1)
                with pool.Fori(1, U_GATE // 2 + 1) as i:
                    low(l, i, 0)
                    low(l, i, 1)
                with pool.Fori(0, GROUPS) as g:
                    st = Step(l, "ssd", g)
                    wait(pool, S_["x_tok"], (l + 1) * TOTAL["x_tok"])
                    wait(pool, S_["dt_a"], l * TOTAL["dt_a"] + 2)
                    wait(pool, S_["y"], l * TOTAL["y"] + g + 1)

                    def chunk(t):
                        yv = y_tok[:, t, bass.ds(g * GW, GW)].rearrange("p (h n) -> p h n", h=HG)

                        def by_head(ap, c):
                            return ap[:, t, bass.ds(g * HG + c, HG)].unsqueeze(2).broadcast_to([P, HG, HD])

                        xt = xdt[:, t].rearrange("p (h n) -> p h n", h=HG)
                        gp.tensor_tensor(xt, yv, by_head(tok, 0), ALU.mult)
                        pool.drain()
                        if t < TB - 1:
                            gp.tensor_tensor(xd[:, t].rearrange("p (h n) -> p h n", h=HG), xt, by_head(dec_tok, 0), ALU.mult)
                        gp.tensor_tensor(yv, yv, par[:, bass.ds(g * HG + C_DSK, HG)].unsqueeze(2).broadcast_to([P, HG, HD]),
                                         ALU.mult)

                    for t in range(TB):
                        chunk(t)
                    pool.drain().then_inc(S_["xd"], 3)
                    low(l, g + (U_GATE // 2 + 1), 0)
                    low(l, g + (U_GATE // 2 + 1), 1)
                with pool.Fori(0, 2) as i:
                    st = Step(l, "z", i)
                    for gg in range(2):
                        for slot in range(2):
                            low(l, i * 4 + (U_ZS // 2 + gg + 1), slot)
                        rsqrt(y_ms, y_rs, st, "y_ms", "y_rs")
                    for u in range(4):
                        low(l, i * 4 + (U_ZS // 2 + 3 + u // 2), u % 2)
                with pool.Fori(0, 2) as i:
                    st = Step(l, "att", i)
                    for pair in range(2):
                        for u in range(3):
                            n = 3 * pair + u
                            low(l, i * 3 + (U_QKV // 2 + n // 2 + 1), n % 2)
                        for h in range(2):
                            rsqrt(y_ms, y_rs, st, "o_ms", "o_rs")
                st = Step(l, "mix")
                for nh in range(U_AO // 2 + 1, U_FF // 2 + 1):
                    low(l, nh, 0)
                    low(l, nh, 1)
                rsqrt(ms, rs, st, "ms", "rs")
                with pool.Fori(U_FF // 2 + 1, UNITS_H) as i:
                    low(l, i, 0)
                    low(l, i, 1)
            rsqrt(ms, rs, Step(DEPTH, "start"), "ms", "rs")

        def y_low(st, i, gg, q):
            wait(nc.vector, S_["y_hi"], st("y_hi") + 1)
            nc.vector.scalar_tensor_tensor(
                op_lo[:, 4 * gg + q, :], ab[q % 2][:], par[:, bass.ds(i * 8 + (C_SNG + 4 * gg + q), 1)],
                op_hi[:, 4 * gg + q, :].bitcast(F32), ALU.mult, ALU.subtract).then_inc(aux_free[q % 2], 1)
            nc.vector.drain().then_inc(S_["y_lo"], 1)

        block = ctx.enter_context(nc.Block())

        @block.sync
        def _(sp):
            sp_program(sp)

        @block.tensor
        def _(pe):
            pe_program(pe)

        @block.scalar
        def _(act):
            act_program(act)

        @block.vector
        def _(dve):
            dve_program(dve)

        @block.gpsimd
        def _(pool):
            pool_program(pool)


def _units(w):
    w = w.reshape(-1, KB, P, w.shape[1] // UW, UW)
    return w.transpose(0, 3, 2, 1, 4).reshape(-1, P, KB * UW)


def _blocks(v):
    return v.reshape(-1, P).T


def _layer_stream(a, l):
    w = a["w_in"][l]
    o = np.cumsum([0, DI, DI, 2 * GROUPS * STATE, HEADS, 2 * AH * AD, 2 * AH * AD, 2 * AH * AD, D, D])
    z, xs, bc, dt, q, k, v, gs, ga = (w[:, o[n]:o[n + 1]] for n in range(9))
    zu, so = _units(z), _units(a["w_ssm_out"][l])
    qu, ku, vu = _units(q), _units(k), _units(v)
    f1, f2 = _units(a["w_ff1"][l]), _units(a["w_ff2"][l])
    parts = [_units(a["w_ada"][l]), _units(bc), _units(xs), _units(gs), _units(ga)]
    for i in range(2):
        parts += [zu[4 * i:4 * i + 4], so[4 * i:4 * i + 4]]
    for p in range(4):
        parts += [qu[p:p + 1], ku[p:p + 1], vu[p:p + 1]]
    parts += [_units(a["w_attn_out"][l]), _units(a["w_out"][l])]
    for i in range(4):
        parts += [f1[4 * i:4 * i + 4], f2[4 * i:4 * i + 4]]
    dtw = np.zeros((P, KB, P), w.dtype)
    dtw[:, :, 0:HEADS] = dt.reshape(KB, P, HEADS).transpose(1, 0, 2)
    return np.concatenate(parts), dtw.reshape(P, KB * P)


def _layer_params(a, l):
    par = np.zeros((P, NPAR), np.float32)
    order = np.concatenate([np.arange(DI, DI + 2 * GROUPS * STATE), np.arange(DI)])
    par[:, C_N1:C_N1 + KB] = _blocks(a["norm1_g"][l])
    par[:, C_CW:C_CB] = a["conv_w"][l][:, order].reshape(CONV, CONV_BLOCKS, P).transpose(2, 1, 0).reshape(P, -1)
    par[:, C_CB:C_DSK] = _blocks(a["conv_b"][l][order])
    par[:, C_DSK:C_SNG] = a["d_skip"][l][None]
    par[:, C_SNG:C_SUB] = _blocks(a["ssm_norm_g"][l])
    par[:, C_SUB] = a["subln_g"][l]
    par[:, C_LAM:C_BADA] = np.concatenate([a[n][l] for n in ("lam_q1", "lam_k1", "lam_q2", "lam_k2")])[None]
    par[:, C_BADA:C_N2] = _blocks(a["b_ada"][l])
    par[:, C_N2:C_DTB] = _blocks(a["norm2_g"][l])
    par[0:HEADS, C_DTB] = a["dt_bias"][l]
    par[0:HEADS, C_ALOG] = a["a_log"][l]
    init = 0.8 - 0.6 * float(np.exp(-0.3 * l))
    par[:, C_LI], par[:, C_OML] = init, 1.0 - init
    return par


def _consts(a):
    con = np.zeros((P, NCON), np.float32)
    con[:, K_C:K_FG] = _blocks(a["c"][0])
    con[:, K_FG:K_ID] = _blocks(a["final_g"])
    con[:, K_ID:K_TRI] = np.eye(P)
    con[:, K_TRI:K_NEG] = np.triu(np.ones((P, P)))
    con[:, K_NEG:K_SEL] = np.where(np.tri(P) > 0, 0.0, -1e30)
    con[0:2 * HEADS, K_SEL:] = np.tile(np.eye(HEADS), (2, 1))
    inv = (1.0 / (np.float32(10000.0) ** (np.arange(0, AD, 2, dtype=np.float32) / np.float32(AD)))).astype(np.float32)
    ang = (np.arange(S, dtype=np.float32)[:, None] * inv[None, :]).astype(np.float32)
    cos, sin = np.cos(ang).T, np.sin(ang).T
    ropes = np.stack([np.tile(cos, (4, 1)), np.concatenate([-sin, sin, -sin, sin])]).astype(np.float32)
    return con, ropes


def kernel(**inputs):
    import concourse.bacc as bacc
    from concourse.bass_utils import run_bass_kernel_spmd

    a = {k: np.asarray(v) for k, v in inputs.items()}
    streams, dtws = zip(*(_layer_stream(a, l) for l in range(DEPTH)))
    con, ropes = _consts(a)
    arrays = {
        "stream": np.concatenate(streams),
        "dtw": np.stack(dtws),
        "params": np.stack([_layer_params(a, l) for l in range(DEPTH)]),
        "consts": con,
        "ropes": ropes,
        "xT": np.ascontiguousarray(a["x"][0].T.reshape(KB, P, S).transpose(1, 0, 2)),
    }
    nc = bacc.Bacc("TRN2", target_bir_lowering=False, num_devices=1)
    args = [nc.dram_tensor(n, v.shape, F32, kind="ExternalInput").ap() for n, v in arrays.items()]
    args.append(nc.dram_tensor("xsave", [P, KB, S], F32, kind="Internal").ap())
    args.append(nc.dram_tensor("out", [P, KB, S], F32, kind="ExternalOutput").ap())
    build(nc, *args)
    r = run_bass_kernel_spmd(nc, [arrays], core_ids=[0])
    y = r.results[0]["out"]
    return np.ascontiguousarray(y.transpose(1, 0, 2).reshape(D, S).T).reshape(1, S, D)
```

```python
from contextlib import ExitStack

import numpy as np

import concourse.bass as bass
from concourse import mybir

F32 = mybir.dt.float32
F32R = mybir.dt.float32r
ALU = mybir.AluOpType
ACT = mybir.ActivationFunctionType
AX_X = mybir.AxisListType.X

P = 128
DEPTH, D, S = 2, 1024, 512
KB = D // P
TB = S // P
DI = 2 * D
GROUPS, STATE, HD = 4, 128, 64
HEADS = DI // HD
HG = HEADS // GROUPS
GW = DI // GROUPS
AH, AD = 8, 64
FF = 4 * D
CONV = 4
CONV_BLOCKS = (DI + 2 * GROUPS * STATE) // P
EPS = 1e-5
UW = 256

N_BC, N_XS, N_GATE, N_ZS, N_QKV, N_AO, N_WO, N_FF = 4, 8, 8, 16, 12, 4, 4, 32
U_BC = 0
U_XS = U_BC + N_BC
U_GATE = U_XS + N_XS
U_ZS = U_GATE + N_GATE
U_QKV = U_ZS + N_ZS
U_AO = U_QKV + N_QKV
U_WO = U_AO + N_AO
U_FF = U_WO + N_WO
UNITS = U_FF + N_FF
ADA = 6 * D // UW
PIECES = ADA + UNITS
ADA_H, ADA_Q, UNITS_H = ADA // 2, ADA // 4, UNITS // 2
SLOT_LOADS = ADA_Q + UNITS_H

C_N1, C_CW, C_CB = 0, 8, 8 + CONV * CONV_BLOCKS
C_DSK = C_CB + CONV_BLOCKS
C_SNG = C_DSK + HEADS
C_SUB = C_SNG + DI // P
C_LAM = C_SUB + 1
C_BADA = C_LAM + 4 * AD
C_N2 = C_BADA + 6 * KB
C_DTB = C_N2 + KB
C_ALOG = C_DTB + 1
C_LI = C_ALOG + 1
C_OML = C_LI + 1
NPAR = C_OML + 1
K_C, K_FG, K_ID = 0, KB, 2 * KB
K_TRI, K_NEG = K_ID + P, K_ID + 2 * P
K_SEL = K_NEG + P
NCON = K_SEL + HEADS

NORM = {"sq": 8, "sq_used": 8, "ss": 1, "ms": 1, "rs": 1, "pre": 8, "h_hi": 8, "h_lo": 8, "bank0": 1, "bank1": 1}
PHASES = [
    ("start", 1, {**NORM, "bank2": 1, "bank3": 1, "bank0": 2, "lam": 2, "dtw": 2, "dt_a": 2, "dt_v": 1, "x_tok": 1}),
    ("bc", 2, {"seed": 4, "taps": 4, "tanh": 4, "silu": 4}),
    ("xs", 4, {"seed": 4, "taps": 4, "tanh": 4, "silu": 4, "bank0": 2, "bank1": 2}),
    ("ssd", 4, {"bc_copy": 1, "cb": 1, "b_tok": 1, "bank0": 8, "bank1": 5, "bank2": 4, "bank3": 4, "seg": 8,
                "sum": 8, "cdec": 1, "m": 8, "m_used": 8, "xdt": 1, "xd": 1, "dx": 1, "state": 3}),
    ("z", 2, {"z_act": 8, "z_used": 9, "y_gate": 2, "y_sq": 2, "y_ms": 2, "y_rs": 2, "yn": 8,
              "y_hi": 8, "y_lo": 8, "bank0": 4, "bank1": 4}),
    ("att", 1, {"swap": 16, "rope": 16, "v": 4, "bank0": 32, "bank1": 32, "bank2": 40, "bank3": 8,
                "mx": 32, "e": 32, "p": 32, "pt": 32, "o_sq": 8, "o_ms": 8, "o_rs": 8, "on": 8, "o_hi": 8,
                "o_lo": 8}),
    ("mix", 1, {**NORM, "mixed": 1, "x_sum": 1, "mix_hi": 8, "mix_lo": 8}),
    ("ff", 4, {"relu": 8, "u_hi": 8, "u_lo": 8}),
    ("end", 1, {"layer": 1}),
]
PAIRS = AH // 2
ATT = [(pair, h, j) for pair in range(PAIRS) for h in range(2) for j in range(TB)]
TOTAL, BASE = {}, {}
for _phase, _rounds, _signals in PHASES:
    for _name, _n in _signals.items():
        BASE[_phase, _name] = TOTAL.get(_name, 0)
        TOTAL[_name] = TOTAL.get(_name, 0) + _rounds * _n
PER = {phase: signals for phase, _, signals in PHASES}


class Step:

    def __init__(self, layer, phase, i=0):
        self.layer, self.phase, self.i, self.seen = layer, phase, i, {}

    def __call__(self, name):
        k = self.seen.get(name, 0)
        self.seen[name] = k + 1
        return self.at(name, k)

    def at(self, name, k):
        per = PER[self.phase][name]
        base = BASE[self.phase, name]
        if isinstance(self.i, int):
            return self.layer * TOTAL[name] + (base + self.i * per + k)
        return self.layer * TOTAL[name] + self.i * per + (base + k)

    def end(self):
        for name, k in self.seen.items():
            assert k == PER[self.phase][name], (self.phase, name, k)


def build(nc, stream, dtw, params, consts, ropes, xT, xsave, out):
    ctx = ExitStack()
    with ctx:
        at = [nc.sbuf_base + (-nc.sbuf_base) % 32]
        ctx.enter_context(nc.sbuf_tensor("arena", [P, 212000 // 4], F32))

        def place(name, shape, dt, offset):
            return nc.alloc_sbuf_tensor_at(name, shape, dt, offset=offset)

        def region(nbytes):
            o = at[0]
            at[0] += nbytes + (-nbytes) % 32
            return o

        K16 = KB * S * 4
        T2 = S * 4
        r_raw, r_hi, r_lo = region(K16), region(K16), region(K16)
        raw = place("raw", [P, 2, KB, UW], F32, r_raw)
        w_hi = place("w_hi", [P, 2, KB, UW], F32R, r_hi)
        w_lo = place("w_lo", [P, 2, KB, UW], F32R, r_lo)
        h_hi = place("h_hi", [P, KB, S], F32R, region(K16))
        h_lo = place("h_lo", [P, KB, S], F32R, region(K16))
        r_op = region(2 * K16)
        op_hi = place("op_hi", [P, KB, S], F32R, r_op)
        op_lo = place("op_lo", [P, KB, S], F32R, r_op + K16)
        r_x = region(K16)
        bct = place("bct", [P, 2 * GROUPS, S], F32, r_x)
        mix = place("mix", [P, KB, S], F32, r_x)
        r_a = region(2 * K16)
        y_tok = place("y_tok", [P, TB, DI], F32, r_a)
        x = place("x", [P, KB, S], F32, r_a + K16)
        r_g = region(2 * K16)
        gates = place("gates", [P, 2 * KB, S], F32, r_g)
        gate_s, gate_a = gates[:, 0:KB], gates[:, KB:2 * KB]

        sq = place("sq", [P, 2, S], F32, r_op)
        ss = place("ss", [P, S], F32, r_op + 2 * T2)
        pre = place("pre", [P, 2, S], F32, r_op + 3 * T2)
        conv = place("conv", [P, 4, S], F32, r_op)
        ctanh = place("ctanh", [P, 4, S], F32, r_op + 4 * T2)
        xsf = place("xsf", [P, 4, S], F32, r_op + 8 * T2)
        bg = place("bg", [P, S], F32, r_op)
        cg = place("cg", [P, S], F32, r_op + T2)
        b_tok = place("b_tok", [P, TB, STATE], F32, r_op + 2 * T2)
        cbm = place("cbm", [P, TB, P], F32, r_op + 3 * T2)
        decayed = place("decayed", [P, 2, TB, P], F32, r_op + 4 * T2)
        xdt = place("xdt", [P, TB, GW], F32, r_op + 6 * T2)
        xd = place("xd", [P, TB - 1, GW], F32, r_op + 10 * T2)
        state = place("state", [P, 2, GW], F32, r_op + 13 * T2)
        y_off = place("y_off", [P, GW], F32, r_op + 15 * T2)

        ada_acc = place("ada_acc", [P, 2, UW], F32, r_g)
        ada_rows = place("ada_rows", [1, ADA_H * UW], F32, r_g + 7 * T2)
        dtw_raw = place("dtw_raw", [P, KB, P], F32, r_g + T2)
        dtw_hi = place("dtw_hi", [P, KB, P], F32R, r_g + 3 * T2)
        dtw_lo = place("dtw_lo", [P, KB, P], F32R, r_g + 5 * T2)
        dt_x = place("dt_x", [HEADS, S], F32, r_g + 7 * T2)
        dt_e = place("dt_e", [HEADS, S], F32, r_g + 8 * T2)
        dt_s = place("dt_s", [HEADS, S], F32, r_g + 9 * T2)
        dt_s2 = place("dt_s2", [HEADS, S], F32, r_g + 10 * T2)
        dt_p = place("dt_p", [HEADS, S], F32, r_g + 11 * T2)
        dt_one = place("dt_one", [HEADS, S], F32, r_g + 12 * T2)
        dt_cum = place("dt_cum", [HEADS, S], F32, r_g + 13 * T2)
        dt_rows = place("dt_rows", [3 * HEADS, S], F32, r_g + 14 * T2)

        ada_raw = place("ada_raw", [P, 2, KB, UW], F32, r_a)
        qT = place("qT", [P, 2, 2, S], F32, r_a)
        kT = place("kT", [P, 2, 2, S], F32, r_a + 4 * T2)
        v_tok = place("v_tok", [P, 2, TB, UW], F32, r_a + 8 * T2)
        swap = place("swap", [P, 2, S], F32, r_a + 12 * T2)
        qc = place("qc", [P, S], F32, r_a + 14 * T2)
        probs = place("probs", [P, 2, 2, S], F32, r_g)
        probsT = place("probsT", [P, 2, S], F32, r_g + 4 * T2)
        o_n = place("o_n", [P, TB, P], F32, r_g + 6 * T2)
        relu = place("relu", [P, 4, S], F32, r_g)
        usq = place("usq", [P, 2, S], F32, r_g + 4 * T2)
        y_out = place("y_out", [P, KB, S], F32, r_g + K16)

        r_z = region(3 * T2)
        zt = place("zt", [P, 2, UW], F32, r_z)
        zh = place("zh", [P, 2, UW], F32, r_z + T2)
        yn = place("yn", [P, TB, P], F32, r_z + 2 * T2)
        seg = place("seg", [P, 2, TB, P], F32, r_z)
        rope_cos = place("rope_cos", [P, S], F32, r_z)
        rope_sin = place("rope_sin", [P, S], F32, r_z + T2)

        def small(name, cols, dt=F32, rows=P):
            return place(name, [rows, cols], dt, region(cols * 4))

        con = small("con", NCON)
        par = small("par", NPAR)
        ident = con[:, K_ID:K_ID + P]
        first = small("first", 2 + 3 * KB)
        ones, cact, g1h = first[:, 0:2], first[:, 2:2 + 2 * KB], first[:, 2 + 2 * KB:2 + 3 * KB]
        ada = small("ada", 6 * KB)
        ada_v = ada[:, :].rearrange("p (a k) -> p a k", a=6)
        cw = small("cw", (CONV + 1) * CONV_BLOCKS)
        amul = small("amul", 2 * KB)
        lamw = small("lamw", 2 * AD)
        odd = small("odd", 8)
        lams, a_neg, subg = odd[:, 0:4], odd[:, 4:6], odd[:, 6:7]
        acum = small("acum", S, F32R, 2 * HEADS)
        selg = small("selg", HG, F32R, 2 * HEADS)
        tok = place("tok", [P, TB, 3 * HEADS], F32, region(TB * 3 * HEADS * 4))
        ea_tok = place("ea_tok", [P, TB, HEADS], F32, region(TB * HEADS * 4))
        dec_tok = place("dec_tok", [P, TB, HEADS], F32, region(TB * HEADS * 4))
        cdec = place("cdec", [P, HG, TB], F32, region(HG * TB * 4))
        smalls = small("smalls", 9 * 4)
        ms, rs, y_ms, y_rs, half,\
            mxs, mxn, den, rden = (smalls[:, 4 * n:4 * n + 4] for n in range(9))
        assert at[0] <= nc.sbuf_usable_end, (at[0], nc.sbuf_usable_end)

        def ps(name):
            return ctx.enter_context(nc.psum_tensor(name, [P, S], F32))

        gb = [ps(f"gemm{b}") for b in range(4)]
        ab = [ps(f"aux{b}") for b in range(4)]

        def sem(name):
            return ctx.enter_context(nc.semaphore(name))

        raw_in = [sem("raw_in0"), sem("raw_in1")]
        hi_ready, lo_ready = sem("hi_ready"), sem("lo_ready")
        gemm_done = sem("gemm_done")
        bank_free = [sem("bank_free0"), sem("bank_free1")]
        aux_full = [sem(f"aux_full{b}") for b in range(4)]
        aux_free = [sem(f"aux_free{b}") for b in range(4)]
        ada_in = [sem("ada_in0"), sem("ada_in1")]
        ada_step, ada_out = sem("ada_step"), sem("ada_out")
        ada_row, ada_kept = sem("ada_row"), sem("ada_kept")
        con_in, par_in, dtw_in, x_in = sem("con_in"), sem("par_in"), sem("dtw_in"), sem("x_in")
        x_saved, x_back, rope_in, out_done = sem("x_saved"), sem("x_back"), sem("rope_in"), sem("out_done")
        ready = sem("ready")
        c_tanh, cact_ready = sem("c_tanh"), sem("cact_ready")
        S_ = {name: sem("s_" + name) for name in TOTAL if not name.startswith("bank")}

        LO_CREDIT, DONE_CREDIT, BANK_CREDIT, AUX_CREDIT, LAYER_CREDIT = 1, 4, 2, 1, 1
        SILU_CREDIT, U_CREDIT, ROPE_CREDIT, Z_CREDIT, M_CREDIT, ROW_CREDIT = 4, 4, 2, 1, HG, 2

        def total_at(l, phase, name, k):
            return l * TOTAL[name] + (BASE[phase, name] + k)

        def done_at(l, n, j):
            return l * (2 * UNITS) + n * 2 + (j + 1 + DONE_CREDIT)

        def raw_at(l, nh):
            return (l * SLOT_LOADS + nh + 1) * 16

        def sp_program(sp):
            sp.dma_start(con[:], consts).then_inc(con_in, 16)
            sp.dma_start(x[:], xT).then_inc(x_in, 16)
            with sp.Fori(0, DEPTH) as l:
                def load_ada(piece, slot):
                    sp.dma_start(ada_raw[:, slot], stream[bass.ds(l * PIECES + piece, 1)].rearrange(
                        "u p (k n) -> p (u k) n", k=KB)).then_inc(ada_in[slot], 16)

                def load(piece, slot):
                    sp.dma_start(raw[:, slot], stream[bass.ds(l * PIECES + piece, 1)].rearrange(
                        "u p (k n) -> p (u k) n", k=KB)).then_inc(raw_in[slot], 16)

                for slot in range(2):
                    load_ada(2 * slot, slot)
                sp.wait_ge(S_["layer"], l + LAYER_CREDIT)
                sp.dma_start(par[:], params[bass.ds(l, 1)].rearrange("l p n -> p (l n)")).then_inc(par_in, 16)
                sp.dma_start(dtw_raw[:], dtw[bass.ds(l, 1)].rearrange("l p (k n) -> p (l k) n", k=KB)).then_inc(dtw_in, 16)
                for slot in range(2):
                    sp.wait_ge(lo_ready, l * UNITS + LO_CREDIT)
                    load(2 * slot + 1, slot)
                with sp.Fori(1, ADA_Q) as i:
                    for slot in range(2):
                        sp.wait_ge(ada_step, (l * ADA_H + i * 2 + (slot - 1)) * KB)
                        load_ada(i * 4 + 2 * slot, slot)
                        sp.wait_ge(ada_row, l * ADA_H + i * 2 + (slot - 1))
                        load(i * 4 + (2 * slot + 1), slot)
                for slot in range(2):
                    sp.wait_ge(ada_row, l * ADA_H + (ADA_H - 1 + slot))
                    load(ADA + slot, slot)
                sp.wait_ge(x_in, 16)
                sp.dma_start(xsave, x[:]).then_inc(x_saved, 16)

                def units(i):
                    for slot in range(2):
                        sp.wait_ge(lo_ready, l * UNITS + i * 2 + (slot - 1 + LO_CREDIT))
                        load(i * 2 + (ADA + slot), slot)

                with sp.Fori(1, U_QKV // 2 + 1) as i:
                    units(i)
                sp.wait_ge(S_["z_used"], total_at(l, "z", "z_used", 2 * 9 + Z_CREDIT))
                sp.dma_start(rope_cos[:], ropes[0]).then_inc(rope_in, 16)
                sp.dma_start(rope_sin[:], ropes[1]).then_inc(rope_in, 16)
                with sp.Fori(U_QKV // 2 + 1, U_AO // 2 + 2) as i:
                    units(i)
                sp.wait_ge(S_["o_lo"], total_at(l, "att", "o_lo", AH))
                sp.dma_start(x[:], xsave).then_inc(x_back, 16)
                with sp.Fori(U_AO // 2 + 2, UNITS_H) as i:
                    units(i)
            sp.wait_ge(S_["pre"], DEPTH * TOTAL["pre"] + KB)
            sp.dma_start(out, y_out[:]).then_inc(out_done, 16)
            sp.wait_ge(out_done, 16)

        def pe_program(pe):
            mm = nc.tensor.matmul
            pe.sem_inc(gemm_done, DONE_CREDIT)
            pe.wait_ge(con_in, 16)
            pe.wait_ge(ready, 1)

            def aux(step, b):
                pe.wait_ge(aux_free[b], step(f"bank{b}") + AUX_CREDIT)
                return ab[b]

            def open_unit(l, nh, slot):
                pe.wait_ge(lo_ready, l * UNITS + nh * 2 + (slot + 1 + LO_CREDIT))
                pe.wait_ge(bank_free[slot], (l * UNITS_H + nh) * 2 + BANK_CREDIT)

            def unit_rows(slot, k, hi, lo):
                for j in range(2):
                    o = gb[2 * slot + j][:]
                    cols = slice(j * P, (j + 1) * P)
                    mm(o, w_hi[:, slot, k, cols], hi[:, k, :], start=k == 0, stop=False)
                    mm(o, w_hi[:, slot, k, cols], lo[:, k, :], start=False, stop=False)
                    last = mm(o, w_lo[:, slot, k, cols], hi[:, k, :], start=False, stop=k == KB - 1)
                    if k == KB - 1:
                        last.then_inc(gemm_done, 1)

            def unit(l, nh, slot, hi, lo, ready_k=None):
                open_unit(l, nh, slot)
                for k in range(KB):
                    if ready_k:
                        ready_k(k)
                    unit_rows(slot, k, hi, lo)

            def unit_tok_half(slot, t, half_k):
                o = gb[2 * slot + t // 2][:, (t % 2) * UW:(t % 2 + 1) * UW]
                toks = slice(t * P, (t + 1) * P)
                for k in range(half_k * KB // 2, (half_k + 1) * KB // 2):
                    mm(o, h_hi[:, k, toks], w_hi[:, slot, k, :], start=k == 0, stop=False)
                    mm(o, h_lo[:, k, toks], w_hi[:, slot, k, :], start=False, stop=False)
                    last = mm(o, h_hi[:, k, toks], w_lo[:, slot, k, :], start=False, stop=k == KB - 1)
                if t % 2 and half_k:
                    last.then_inc(gemm_done, 1)

            def unit_tok(l, nh, slot):
                open_unit(l, nh, slot)
                for t in range(TB):
                    unit_tok_half(slot, t, 0)
                    unit_tok_half(slot, t, 1)

            def transposes(bank, source, rows=P, cols=P, n=TB):
                for t in range(n):
                    last = nc.tensor.transpose(bank[0:cols, t * P:t * P + rows], source(t), ident[0:rows, 0:rows])
                return last

            def norm(step):
                pe.wait_ge(S_["ss"], step("ss") + 1)
                b = aux(step, 0)
                for t in range(TB):
                    last = mm(b[:, t:t + 1], ss[:, t * P:(t + 1) * P], ones[:, 0:1], start=True, stop=True)
                last.then_inc(aux_full[0], 1)
                pe.wait_ge(S_["rs"], step("rs") + 1)
                b = aux(step, 1)
                for t in range(TB):
                    last = mm(b[:, t * P:(t + 1) * P], rs[:, t:t + 1].broadcast_to([P, P]), ident, start=True, stop=True)
                last.then_inc(aux_full[1], 1)

            with pe.Fori(0, DEPTH) as l:
                st = Step(l, "start")
                norm(st)
                n, b2 = st("bank0"), st("bank2")
                with pe.Fori(0, ADA_H // 2) as i:
                    pe.wait_ge(aux_free[0], n + AUX_CREDIT)
                    pe.wait_ge(aux_free[2], b2 + AUX_CREDIT)
                    pe.wait_ge(aux_free[3], st.at("bank3", 0) + AUX_CREDIT)
                    for s in range(2):
                        pe.wait_ge(raw_in[s], raw_at(l, i))
                        pe.wait_ge(ada_kept, l * ADA_H + i * 2 + (s + 1))
                        for k in range(KB):
                            last = mm(ab[2 + s][0:1, 0:UW], cact[:, k:k + 1], raw[:, s, k, :],
                                      start=k == 0, stop=k == KB - 1)
                        last.then_inc(ada_row, 1)
                        pe.wait_ge(ada_step, (l * ADA_H + i * 2 + (s + 1)) * KB)
                        for j in range(2):
                            last = mm(ab[0][:, bass.ds(i * 8 + (4 * s + j), 1)], ada_acc[:, s, j * P:(j + 1) * P],
                                      ones[:, 0:1], start=True, stop=True)
                        last.then_inc(ada_out, 1)
                pe.wait_ge(ada_kept, l * ADA_H + (ADA_H + ROW_CREDIT))
                for m in range(ADA_H):
                    for j in range(2):
                        c = (2 * m + 1) * 2 + j
                        mm(ab[0][:, c:c + 1], ada_rows[0:1, m * UW + j * P:m * UW + (j + 1) * P], ones[0:1, 0:1],
                           start=True, stop=True)
                pe.drain().then_inc(aux_full[0], 1)

                b = ab[2]
                pe.wait_ge(S_["dtw"], st.at("dtw", 1) + 1)
                for k in range(KB):
                    pe.wait_ge(S_["h_lo"], st.at("h_lo", k) + 1)
                    mm(b[:], dtw_hi[:, k, :], h_hi[:, k, :], start=k == 0, stop=False)
                    mm(b[:], dtw_hi[:, k, :], h_lo[:, k, :], start=False, stop=False)
                    last = mm(b[:], dtw_lo[:, k, :], h_hi[:, k, :], start=False, stop=k == KB - 1)
                last.then_inc(aux_full[2], 1)

                def dt_to_tokens():
                    b = aux(st, 3)
                    pe.wait_ge(S_["dt_v"], st("dt_v") + 1)
                    for t in range(TB):
                        last = nc.tensor.transpose(b[:, t * P:t * P + 3 * HEADS], dt_rows[:, t * P:(t + 1) * P],
                                                   ident[0:3 * HEADS, 0:3 * HEADS])
                    last.then_inc(aux_full[3], 1)
                    st.end()

                with pe.Fori(0, N_BC // 2) as i:
                    for slot in range(2):
                        unit(l, i + U_BC // 2, slot, h_hi, h_lo)

                def turn_xs(i, s):
                    step = Step(l, "xs", i)
                    for j in range(2):
                        pe.wait_ge(S_["silu"], step.at("silu", 2 * s + j) + (1 + SILU_CREDIT))
                        pe.wait_ge(aux_free[j], step.at(f"bank{j}", s) + AUX_CREDIT)
                        transposes(ab[j], lambda t: xsf[:, 2 * s + j, t * P:(t + 1) * P]).then_inc(aux_full[j], 1)

                def xs_round(i, first):
                    unit(l, i + U_XS // 2, 0, h_hi, h_lo)
                    if not first:
                        turn_xs(i - 1, 1)
                    unit(l, i + U_XS // 2, 1, h_hi, h_lo)
                    turn_xs(i, 0)

                xs_round(0, True)
                dt_to_tokens()
                with pe.Fori(1, N_XS // 2) as i:
                    xs_round(i, False)
                turn_xs(N_XS // 2 - 1, 1)

                with pe.Fori(0, GROUPS) as g:
                    st = Step(l, "ssd", g)

                    def spread(r):
                        b = aux(st, 2 + r % 2)
                        mm(b[:], selg[:, r:r + 1].broadcast_to([2 * HEADS, P]), acum[:], start=True, stop=True)\
                            .then_inc(aux_full[2 + r % 2], 1)

                    def diagonal(r, b):
                        if r == 0:
                            pe.wait_ge(S_["xdt"], st("xdt") + 1)
                        pe.wait_ge(S_["m"], st("m") + 1)
                        for t in range(TB):
                            last = mm(b[:, t * P + (r % 2) * HD:t * P + (r % 2 + 1) * HD], decayed[:, r % 2, t, :],
                                      xdt[:, t, r * HD:(r + 1) * HD], start=True, stop=True)
                        last.then_inc(S_["m_used"], 1)
                        st("m_used")

                    def chunk_state(t):
                        b = aux(st, 0)
                        if t == 0:
                            pe.wait_ge(S_["xd"], st("xd") + 1)
                            pe.wait_ge(S_["b_tok"], st("b_tok") + 1)
                        mm(b[:], b_tok[:, t, :], xd[:, t, :], start=True, stop=True).then_inc(aux_full[0], 1)

                    def off_diagonal(t):
                        b = aux(st, 0)
                        pe.wait_ge(S_["state"], st("state") + 1)
                        mm(b[:], cg[:, t * P:(t + 1) * P], state[:, (t - 1) % 2, :], start=True, stop=True)\
                            .then_inc(aux_full[0], 1)

                    def gate_parts(first, last):
                        for part in range(first, last):
                            slot, k = divmod(part, KB)
                            if k == 0:
                                open_unit(l, g + U_GATE // 2, slot)
                            unit_rows(slot, k, h_hi, h_lo)

                    gate_parts(0, 1)
                    pe.wait_ge(S_["bc_copy"], st("bc_copy") + 1)
                    b = aux(st, 0)
                    for r in range(HG):
                        last = mm(b[:, r * TB:(r + 1) * TB], selg[:, r:r + 1].broadcast_to([2 * HEADS, P]),
                                  acum[:, P - 1:S:P], start=True, stop=True)
                    last.then_inc(aux_full[0], 1)
                    b = aux(st, 0)
                    for t in range(TB):
                        last = mm(b[:, t * P:(t + 1) * P], bg[:, t * P:(t + 1) * P], cg[:, t * P:(t + 1) * P],
                                  start=True, stop=True)
                    last.then_inc(aux_full[0], 1)
                    b = aux(st, 1)
                    transposes(b, lambda t: bg[:, t * P:(t + 1) * P]).then_inc(aux_full[1], 1)
                    spread(0)
                    spread(1)
                    gate_parts(1, 2)
                    part = 2
                    between = {0: (chunk_state, 0), 1: (off_diagonal, 1), 2: (chunk_state, 1),
                               3: (off_diagonal, 2), 4: (chunk_state, 2), 6: (off_diagonal, 3)}
                    for r in range(HG):
                        more = 2 if r < 6 else 1
                        gate_parts(part, part + more)
                        part += more
                        if r % 2 == 0:
                            b = aux(st, 1)
                        diagonal(r, b)
                        if r % 2:
                            pe.drain().then_inc(aux_full[1], 1)
                        if r + 2 < HG:
                            spread(r + 2)
                        if r in between:
                            step, t = between[r]
                            step(t)
                    st.end()

                with pe.Fori(0, 2) as i:
                    st = Step(l, "z", i)
                    def turn_y(q):
                        b = aux(st, q % 2)
                        pe.wait_ge(S_["yn"], st("yn") + 1)
                        transposes(b, lambda t: yn[:, t, :]).then_inc(aux_full[q % 2], 1)

                    def out_rows(u, ks, opened=False):
                        if not opened:
                            open_unit(l, i * 4 + (U_ZS // 2 + 2 + u // 2), u % 2)
                        for k in ks:
                            if u == 0:
                                pe.wait_ge(S_["y_lo"], st("y_lo") + 1)
                            unit_rows(u % 2, k, op_hi, op_lo)

                    for u in range(3):
                        unit_tok(l, i * 4 + (U_ZS // 2 + u // 2), u % 2)
                    open_unit(l, i * 4 + (U_ZS // 2 + 1), 1)
                    for t in range(TB):
                        unit_tok_half(1, t, 0)
                        unit_tok_half(1, t, 1)
                        turn_y(t)
                    out_rows(0, range(KB // 2))
                    out_rows(1, range(KB // 2))
                    for q in range(4):
                        turn_y(q)
                    out_rows(0, range(KB // 2, KB), True)
                    out_rows(1, range(KB // 2, KB), True)
                    out_rows(2, range(KB))
                    out_rows(3, range(KB))
                    st.end()

                st = Step(l, "att")

                def qkv(pair, part):
                    u, k = divmod(part, KB)
                    n = 3 * pair + u
                    if k == 0:
                        open_unit(l, U_QKV // 2 + n // 2, n % 2)
                    if u < 2:
                        unit_rows(n % 2, k, h_hi, h_lo)
                    else:
                        unit_tok_half(n % 2, k // 2, k % 2)

                def scores(pair, h, j):
                    if h == 0 and j == 0:
                        pe.wait_ge(S_["rope"], st.at("rope", 4 * pair + 3) + (1 + ROPE_CREDIT))
                    for part in range(2):
                        rows = slice(part * AD, (part + 1) * AD)
                        b = aux(st, part)
                        mm(b[:, 0:(j + 1) * P], qT[rows, pair % 2, h, j * P:(j + 1) * P],
                           kT[rows, pair % 2, h, 0:(j + 1) * P], start=True, stop=True).then_inc(aux_full[part], 1)

                def weigh(pair, h, j):
                    if j == 0:
                        aux(st, 3)
                        if h == 0:
                            pe.wait_ge(S_["v"], st("v") + 1)
                    pe.wait_ge(S_["pt"], st("pt") + 1)
                    for t in range(j + 1):
                        last = mm(ab[3][:, j * P:(j + 1) * P], probsT[:, j % 2, t * P:(t + 1) * P],
                                  v_tok[:, pair % 2, t, h * P:(h + 1) * P], start=t == 0, stop=t == j)
                    if j == TB - 1:
                        last.then_inc(aux_full[3], 1)

                def turn_probs(j):
                    b = aux(st, 2)
                    pe.wait_ge(S_["p"], st("p") + 1)
                    transposes(b, lambda t: probs[:, j % 2, 0, t * P:(t + 1) * P], n=j + 1)\
                        .then_inc(aux_full[2], 1)

                def turn_o():
                    b = aux(st, 2)
                    pe.wait_ge(S_["on"], st("on") + 1)
                    transposes(b, lambda t: o_n[:, t, :]).then_inc(aux_full[2], 1)

                for part in range(3 * KB):
                    qkv(0, part)
                scores(*ATT[0])
                for n, (pair, h, j) in enumerate(ATT):
                    part = n % (2 * TB) * 3
                    if n + 1 < len(ATT):
                        scores(*ATT[n + 1])
                    if pair + 1 < PAIRS:
                        qkv(pair + 1, part)
                        qkv(pair + 1, part + 1)
                    turn_probs(j)
                    if pair + 1 < PAIRS:
                        qkv(pair + 1, part + 2)
                    if n:
                        weigh(*ATT[n - 1])
                    if n > TB and n % TB == 1:
                        turn_o()
                weigh(*ATT[-1])
                turn_o()
                st = Step(l, "mix")
                pe.wait_ge(S_["o_lo"], total_at(l, "att", "o_lo", AH))
                for u in range(N_AO):
                    unit(l, U_AO // 2 + u // 2, u % 2, op_hi, op_lo)
                for u in range(N_WO):
                    def mixed(k):
                        if u == 0:
                            pe.wait_ge(S_["mix_lo"], st("mix_lo") + 1)
                    unit(l, U_WO // 2 + u // 2, u % 2, h_hi, h_lo, mixed)
                norm(st)
                with pe.Fori(0, 4) as i:
                    sf = Step(l, "ff", i)
                    for u in range(4):
                        def normed(k):
                            pe.wait_ge(S_["h_lo"], st.at("h_lo", k) + 1)
                        unit(l, i * 4 + (U_FF // 2 + u // 2), u % 2, h_hi, h_lo, normed if u == 0 else None)
                    for u in range(4):
                        def squared(k):
                            if u == 0:
                                pe.wait_ge(S_["u_lo"], sf("u_lo") + (1 + U_CREDIT))
                        unit(l, i * 4 + (U_FF // 2 + 2 + u // 2), u % 2, op_hi, op_lo, squared)
                    sf.end()
                st.end()
            norm(Step(DEPTH, "start"))

        def act_program(act):
            A = nc.scalar.activation

            def convert(l, nh, slot):
                act.wait_ge(raw_in[slot], raw_at(l, nh + ADA_Q))
                act.wait_ge(gemm_done, (l * UNITS + nh * 2) * 2 + (2 * slot + 2))
                A(w_hi[:, slot], raw[:, slot], ACT.Copy).then_inc(hi_ready, 1)

            def full(step, b):
                act.wait_ge(aux_full[b], step(f"bank{b}") + 1)
                return ab[b]

            def squares_of_x(step):
                for k in range(KB):
                    step("sq")
                    if k >= 2:
                        act.wait_ge(S_["sq_used"], step.at("sq_used", k - 2) + 1)
                    A(sq[:, k % 2], x[:, k], ACT.Square).then_inc(S_["sq"], 1)

            def normed_high(step, shift):
                for k in range(KB):
                    act.wait_ge(S_["pre"], step("pre") + 1)
                    A(h_hi[:, k], pre[:, k % 2], ACT.Identity, bias=shift(k)).then_inc(S_["h_hi"], 1)

            act.wait_ge(con_in, 16)
            A(cact[:, KB:2 * KB], con[:, K_C:K_C + KB], ACT.Tanh, scale=0.5).then_inc(c_tanh, 1)
            act.wait_ge(x_in, 16)
            with act.Fori(0, DEPTH) as l:
                st = Step(l, "start")
                act.wait_ge(S_["lam"], st("lam") + 1)
                A(lams[:, 2:4], lams[:, 0:2], ACT.Exp)
                A(a_neg[0:HEADS, 0:1], par[0:HEADS, C_ALOG:C_ALOG + 1], ACT.Exp).then_inc(S_["lam"], 1)
                act.wait_ge(dtw_in, (l + 1) * 16)
                A(dtw_hi[:], dtw_raw[:], ACT.Copy).then_inc(S_["dtw"], 1)
                st("lam"), st("dtw"), st("dtw")
                act.wait_ge(S_["layer"], l + LAYER_CREDIT)

                squares_of_x(st)
                with act.Fori(0, ADA_H // 2) as i:
                    for s in range(2):
                        act.wait_ge(ada_row, l * ADA_H + i * 2 + (s + 1))
                        A(ada_rows[:, bass.ds(i * (2 * UW) + s * UW, UW)], ab[2 + s][0:1, 0:UW], ACT.Copy)\
                            .then_inc(ada_kept, 1)
                normed_high(st, lambda k: ada_v[:, 0, k:k + 1])
                convert(l, 0, 0)
                convert(l, 0, 1)
                b = ab[2]
                act.wait_ge(aux_full[2], st.at("bank2", 0) + 1)
                A(dt_x[:], b[0:HEADS, :], ACT.Identity, bias=par[0:HEADS, C_DTB:C_DTB + 1]).then_inc(aux_free[2], 1)
                act.drain()
                A(dt_e[:], dt_x[:], ACT.Abs)
                act.drain()
                A(dt_e[:], dt_e[:], ACT.Exp, scale=-1.0).then_inc(S_["dt_a"], 1)

                def conv_seed(step, nh, slot, j, block):
                    c = 2 * slot + j
                    act.wait_ge(gemm_done, done_at(l, nh * 2 + slot, j))
                    act.wait_ge(S_["silu"], step.at("silu", c - 4) + (1 + SILU_CREDIT))
                    A(conv[:, c], gb[c][:], ACT.Identity, scale=cw[:, bass.ds(block * CONV + (CONV - 1), 1)],
                      bias=cw[:, bass.ds(block + CONV * CONV_BLOCKS, 1)]).then_inc(S_["seed"], 1)
                    step("seed")

                def conv_tanh(step, c):
                    act.wait_ge(S_["taps"], step("taps") + 1)
                    A(ctanh[:, c], conv[:, c], ACT.Tanh).then_inc(S_["tanh"], 1)
                    step("tanh")

                with act.Fori(0, N_BC // 2) as i:
                    step = Step(l, "bc", i)
                    for slot in range(2):
                        convert(l, i + 1, slot)
                        for j in range(2):
                            conv_seed(step, i + U_BC // 2, slot, j, i * 4 + (2 * slot + j))
                        for j in range(2):
                            conv_tanh(step, 2 * slot + j)
                    step.end()

                def x_to_tok(i, s):
                    step = Step(l, "xs", i)
                    for j in range(2):
                        act.wait_ge(aux_full[j], step.at(f"bank{j}", s) + 1)
                        A(y_tok[:, :, bass.ds(i * (4 * P) + (2 * s + j) * P, P)],
                          ab[j][:].rearrange("p (t n) -> p t n", t=TB), ACT.Copy).then_inc(aux_free[j], 1)

                def xs_round(i, first):
                    step = Step(l, "xs", i)
                    for slot in range(2):
                        convert(l, i + (U_XS // 2 + 1), slot)
                        for j in range(2):
                            conv_seed(step, i + U_XS // 2, slot, j, i * 4 + (2 * N_BC + 2 * slot + j))
                        for j in range(2):
                            conv_tanh(step, 2 * slot + j)
                        if slot == 0 and not first:
                            x_to_tok(i - 1, 1)
                        if slot == 1:
                            x_to_tok(i, 0)

                act.wait_ge(x_saved, (l + 1) * 16)
                xs_round(0, True)
                act.wait_ge(aux_full[3], st.at("bank3", 0) + 1)
                A(tok[:], ab[3][:].rearrange("p (t n) -> p t n", t=TB)[:, :, 0:3 * HEADS], ACT.Copy)\
                    .then_inc(aux_free[3], 1)
                act.drain()
                A(ea_tok[:], tok[:, :, HEADS:2 * HEADS], ACT.Exp, scale=-1.0)
                A(dec_tok[:], tok[:, :, 2 * HEADS:3 * HEADS], ACT.Exp).then_inc(S_["dt_a"], 1)
                with act.Fori(1, N_XS // 2) as i:
                    xs_round(i, False)
                x_to_tok(N_XS // 2 - 1, 1)
                act.drain().then_inc(S_["x_tok"], 1)

                with act.Fori(0, GROUPS) as g:
                    st = Step(l, "ssd", g)
                    act.wait_ge(S_["m_used"], st.at("m_used", -HG) + HG + M_CREDIT)
                    A(bg[:], bct[:, bass.ds(g, 1), :].rearrange("p a n -> p (a n)"), ACT.Copy)
                    A(cg[:], bct[:, bass.ds(g + GROUPS, 1), :].rearrange("p a n -> p (a n)"), ACT.Copy)
                    A(selg[:], con[0:2 * HEADS, bass.ds(g * HG + K_SEL, HG)], ACT.Copy).then_inc(S_["bc_copy"], 1)
                    st("bc_copy")
                    b = full(st, 0)
                    A(cdec[:].rearrange("p h t -> p (h t)"), b[:, 0:HG * TB], ACT.Exp).then_inc(aux_free[0], 1)
                    act.drain().then_inc(S_["cdec"], 1)
                    b = full(st, 1)
                    A(b_tok[:], b[:].rearrange("p (t n) -> p t n", t=TB), ACT.Copy).then_inc(aux_free[1], 1)
                    act.drain().then_inc(S_["b_tok"], 1)

                    def decay(r):
                        act.wait_ge(S_["sum"], st("sum") + 1)
                        tile = seg[:, r % 2].rearrange("p t n -> p (t n)")
                        A(tile, tile, ACT.Relu, scale=-1.0)
                        act.drain()
                        A(tile, tile, ACT.Exp, scale=-1.0).then_inc(S_["seg"], 1)
                        st("seg")

                    def gate(slot):
                        for j in range(2):
                            act.wait_ge(gemm_done, done_at(l, (g + U_GATE // 2) * 2 + slot, j))
                            dst = gates[:, bass.ds(g * 4 + (2 * slot + j), 1), :].rearrange("p a n -> p (a n)")
                            A(dst, gb[2 * slot + j][:], ACT.Tanh, scale=0.5).then_inc(bank_free[slot], 1)

                    for r in range(HG):
                        decay(r)
                        if r == 4:
                            convert(l, g + (U_GATE // 2 + 1), 0)
                            gate(0)
                    convert(l, g + (U_GATE // 2 + 1), 1)
                    gate(1)

                with act.Fori(0, 2) as i:
                    st = Step(l, "z", i)
                    base = U_ZS // 2

                    def tanh_z(u):
                        convert(l, i * 4 + (base + u // 2 + 1), u % 2)
                        for j in range(2):
                            act.wait_ge(gemm_done, done_at(l, (i * 4 + (base + u // 2)) * 2 + u % 2, j))
                            act.wait_ge(S_["z_used"], st.at("z_used", 2 * u + j) + Z_CREDIT)
                            src = gb[2 * (u % 2) + j][:].rearrange("p (t n) -> p t n", t=2)
                            A(zt[:], src, ACT.Tanh, scale=0.5)
                            A(zh[:], src, ACT.Copy, scale=0.5).then_inc(bank_free[u % 2], 1)
                            act.drain().then_inc(S_["z_act"], 1)

                    def squares(gg):
                        act.wait_ge(S_["y_gate"], st("y_gate") + 1)
                        for t in range(TB):
                            A(yn[:].rearrange("p t n -> p (t n)"), y_tok[:, t, bass.ds(i * (2 * GW) + gg * GW, GW)],
                              ACT.Square, accum_out=y_ms[:, t:t + 1])
                            act.drain()
                        act.drain().then_inc(S_["y_sq"], 1)

                    def y_high(gg, q):
                        b = full(st, q % 2)
                        A(op_hi[:, 4 * gg + q, :], b[:], ACT.Copy,
                          scale=par[:, bass.ds(i * 8 + (C_SNG + 4 * gg + q), 1)]).then_inc(S_["y_hi"], 1)

                    tanh_z(0)
                    tanh_z(1)
                    squares(0)
                    y_high(0, 0)
                    y_high(0, 1)
                    tanh_z(2)
                    y_high(0, 2)
                    y_high(0, 3)
                    tanh_z(3)
                    squares(1)
                    for q in range(4):
                        y_high(1, q)
                    for u in range(4):
                        convert(l, i * 4 + (base + 3 + u // 2), u % 2)

                st = Step(l, "att")

                def take_qk(pair, u):
                    n = 3 * pair + u
                    convert(l, U_QKV // 2 + n // 2 + 1, n % 2)
                    for j in range(2):
                        act.wait_ge(gemm_done, done_at(l, U_QKV + n, j))
                        act.wait_ge(S_["rope"], st("rope") + 1)
                        for quarter in range(4):
                            src = quarter ^ 1
                            last = A(swap[quarter * 32:quarter * 32 + 32, j],
                                     gb[2 * (n % 2) + j][src * 32:src * 32 + 32, :], ACT.Copy)
                        last.then_inc(S_["swap"], 1)

                def take_v(pair):
                    n = 3 * pair + 2
                    convert(l, U_QKV // 2 + n // 2 + 1, n % 2)
                    for j in range(2):
                        act.wait_ge(gemm_done, done_at(l, U_QKV + n, j))
                        A(v_tok[:, pair % 2, 2 * j:2 * j + 2, :], gb[2 * (n % 2) + j][:].rearrange("p (t n) -> p t n", t=2),
                          ACT.Copy).then_inc(bank_free[n % 2], 1)
                    act.drain().then_inc(S_["v"], 1)

                def expo(j):
                    act.wait_ge(S_["mx"], st("mx") + 1)
                    for part in range(2):
                        col = 2 * (j % 2) + part
                        A(probs[:, j % 2, part, 0:(j + 1) * P], ab[part][:, 0:(j + 1) * P], ACT.Exp, scale=AD ** -0.5,
                          bias=mxn[:, col:col + 1], accum_out=den[:, col:col + 1]).then_inc(aux_free[part], 1)
                    act.drain().then_inc(S_["e"], 1)

                def probs_out(j):
                    b = full(st, 2)
                    A(probsT[:, j % 2, 0:(j + 1) * P], b[:, 0:(j + 1) * P], ACT.Copy).then_inc(aux_free[2], 1)
                    act.drain().then_inc(S_["pt"], 1)

                def o_square():
                    b = full(st, 3)
                    for t in range(TB):
                        A(o_n[:, t, :], b[:, t * P:(t + 1) * P], ACT.Square, accum_out=y_ms[:, t:t + 1])
                    act.drain().then_inc(S_["o_sq"], 1)

                def o_out(head):
                    b = full(st, 2)
                    A(op_hi[:, head, :], b[:], ACT.Copy, scale=subg[:, 0:1]).then_inc(S_["o_hi"], 1)

                take_qk(0, 0)
                take_qk(0, 1)
                take_v(0)
                expo(0)
                for n, (pair, h, j) in enumerate(ATT):
                    if n + 1 < len(ATT):
                        expo(ATT[n + 1][2])
                    probs_out(j)
                    if n and n % TB == 0:
                        o_square()
                    if n > TB and n % TB == 1:
                        o_out(n // TB - 1)
                    if pair + 1 < PAIRS:
                        if n % (2 * TB) in (2, 5):
                            take_qk(pair + 1, n % (2 * TB) // 3)
                        if n % (2 * TB) == 7:
                            take_v(pair + 1)
                o_square()
                o_out(AH - 1)

                st = Step(l, "mix")
                for u in range(N_AO):
                    convert(l, U_AO // 2 + 1 + u // 2, u % 2)
                for k in range(KB):
                    if k == 0:
                        act.wait_ge(S_["mixed"], st("mixed") + 1)
                    A(h_hi[:, k], mix[:, k], ACT.Copy).then_inc(S_["mix_hi"], 1)
                for u in range(N_WO):
                    convert(l, U_WO // 2 + 1 + u // 2, u % 2)
                act.wait_ge(S_["x_sum"], st("x_sum") + 1)
                squares_of_x(st)
                normed_high(st, lambda k: ada_v[:, 3, k:k + 1])

                def ff_round(i, last_round):
                    sf = Step(l, "ff", i)
                    for u in range(8):
                        if u < 6 or not last_round:
                            convert(l, i * 4 + (U_FF // 2 + u // 2 + 1), u % 2)
                        if u < 4:
                            for j in range(2):
                                act.wait_ge(gemm_done, done_at(l, i * 8 + (U_FF + u), j))
                                c = 2 * (u % 2) + j
                                act.wait_ge(S_["u_lo"], sf.at("u_lo", 2 * u + j - 4) + (1 + U_CREDIT))
                                A(relu[:, c], gb[c][:], ACT.Relu).then_inc(bank_free[u % 2], 1)
                                act.drain().then_inc(S_["relu"], 1)
                                A(op_hi[:, 2 * u + j, :], relu[:, c], ACT.Square).then_inc(S_["u_hi"], 1)
                with act.Fori(0, 3) as i:
                    ff_round(i, False)
                ff_round(3, True)
            act.wait_ge(S_["layer"], DEPTH + LAYER_CREDIT)
            squares_of_x(Step(DEPTH, "start"))

        def dve_program(dve):
            v = nc.vector
            TT, TS, STT = v.tensor_tensor, v.tensor_scalar, v.scalar_tensor_tensor

            def full(step, b):
                dve.wait_ge(aux_full[b], step(f"bank{b}") + 1)
                return ab[b]

            settle = dve.drain

            v.memset(ones[:], 1.0)
            v.memset(half[:], -0.5)
            dve.sem_inc(S_["layer"], LAYER_CREDIT)
            for b in range(4):
                dve.sem_inc(aux_free[b], AUX_CREDIT)
            for s in range(2):
                dve.sem_inc(bank_free[s], BANK_CREDIT)
            dve.sem_inc(S_["m_used"], M_CREDIT)
            dve.sem_inc(ada_kept, ROW_CREDIT)
            dve.sem_inc(S_["silu"], SILU_CREDIT)
            dve.sem_inc(S_["z_used"], Z_CREDIT)
            dve.sem_inc(S_["u_lo"], U_CREDIT)
            dve.sem_inc(S_["rope"], ROPE_CREDIT)
            dve.wait_ge(c_tanh, 1)
            TS(cact[:, 0:KB], con[:, K_C:K_C + KB], 0.5, None, ALU.mult)
            settle()
            STT(cact[:, 0:KB], cact[:, KB:2 * KB], 1.0, cact[:, 0:KB], ALU.add, ALU.mult)
            dve.drain().then_inc(ready, 1)

            def norm_sums(step):
                for k in range(KB):
                    dve.wait_ge(S_["sq"], step("sq") + 1)
                    if k == 0:
                        v.tensor_copy(ss[:], sq[:, 0]).then_inc(S_["sq_used"], 1)
                    else:
                        TT(ss[:], ss[:], sq[:, k % 2], ALU.add).then_inc(S_["sq_used"], 1)
                    settle()
                    step("sq_used")
                dve.drain().then_inc(S_["ss"], 1)
                b = full(step, 0)
                TS(ms[:], b[:, 0:TB], 1.0 / D, EPS, ALU.mult, ALU.add).then_inc(aux_free[0], 1)
                dve.drain().then_inc(S_["ms"], 1)

            def norm(step, mul, shift):
                b = full(step, 1)
                for k in range(KB + 1):
                    if k < KB:
                        if shift is not None and k >= 2:
                            dve.wait_ge(S_["h_hi"], step.at("h_hi", k - 2) + 1)
                        dst = pre[:, k % 2] if shift is not None else y_out[:, k]
                        STT(dst, x[:, k], mul(k), b[:], ALU.mult, ALU.mult).then_inc(S_["pre"], 1)
                        if k == KB - 1:
                            dve.drain().then_inc(aux_free[1], 1)
                    if k and shift is not None:
                        dve.wait_ge(S_["h_hi"], step("h_hi") + 1)
                        STT(h_lo[:, k - 1], pre[:, (k - 1) % 2], shift(k - 1), h_hi[:, k - 1].bitcast(F32), ALU.add,
                            ALU.subtract).then_inc(S_["h_lo"], 1)
                        settle()

            with dve.Fori(0, DEPTH) as l:
                st = Step(l, "start")
                dve.wait_ge(par_in, (l + 1) * 16)
                lv = par[:, C_LAM:C_LAM + 4 * AD].rearrange("p (a b n) -> p a b n", a=2, b=2)
                TT(lamw[:].rearrange("p (a n) -> p a n", a=2), lv[:, :, 0, :], lv[:, :, 1, :], ALU.mult)
                settle()
                v.tensor_reduce(lams[:, 0:2], lamw[:].rearrange("p (a n) -> p a n", a=2), AX_X, ALU.add)\
                    .then_inc(S_["lam"], 1)
                TS(cw[:], par[:, C_CW:C_CW + (CONV + 1) * CONV_BLOCKS], 0.5, None, ALU.mult)
                TT(subg[:], par[:, C_SUB:C_SUB + 1], par[:, C_OML:C_OML + 1], ALU.mult)
                dve.wait_ge(S_["lam"], st.at("lam", 1) + 1)
                TT(lams[:, 1:2], lams[:, 3:4], lams[:, 2:3], ALU.subtract)
                TS(a_neg[0:HEADS, 1:2], a_neg[0:HEADS, 0:1], -1.0, None, ALU.mult)
                settle()
                TT(lams[:, 0:1], lams[:, 1:2], par[:, C_LI:C_LI + 1], ALU.subtract)
                dve.wait_ge(S_["dtw"], st.at("dtw", 0) + 1)
                TT(dtw_lo[:], dtw_raw[:], dtw_hi[:].bitcast(F32), ALU.subtract).then_inc(S_["dtw"], 1)

                norm_sums(st)
                with dve.Fori(0, ADA_H // 2) as i:
                    for s in range(2):
                        dve.wait_ge(ada_in[s], (l * ADA_Q + i + 1) * 16)
                        for k in range(KB):
                            if k == 0:
                                dve.wait_ge(ada_out, l * ADA_H + i * 2 + (s + 1))
                                TS(ada_acc[:, s], ada_raw[:, s, 0], cact[:, 0:1], None, ALU.mult).then_inc(ada_step, 1)
                            else:
                                dve.wait_ge(ada_step, l * (ADA_H * KB) + i * (2 * KB) + (s * KB + k))
                                STT(ada_acc[:, s], ada_raw[:, s, k], cact[:, k:k + 1], ada_acc[:, s], ALU.mult, ALU.add)\
                                    .then_inc(ada_step, 1)
                b = full(st, 0)
                TT(ada[:], b[:, 0:6 * KB], par[:, C_BADA:C_BADA + 6 * KB], ALU.add).then_inc(aux_free[0], 1)
                settle()
                for m, (scale_at, norm_at) in enumerate(((1, C_N1), (4, C_N2))):
                    STT(amul[:, m * KB:(m + 1) * KB], ada_v[:, scale_at, :], 1.0, par[:, norm_at:norm_at + KB],
                        ALU.add, ALU.mult)
                TS(g1h[:], ada_v[:, 2, :], 0.5, None, ALU.mult)
                settle()
                norm(st, lambda k: amul[:, k:k + 1], lambda k: ada_v[:, 0, k:k + 1])

                v.memset(dt_one[:], 1.0)
                dve.wait_ge(S_["dt_a"], st.at("dt_a", 0) + 1)
                TS(dt_s[:], dt_e[:], 2.0, None, ALU.add)
                settle()
                v.reciprocal(dt_s2[:], dt_s[:])
                settle()
                TT(dt_s[:], dt_e[:], dt_s2[:], ALU.mult)
                settle()
                TT(dt_s2[:], dt_s[:], dt_s[:], ALU.mult)
                settle()
                TS(dt_p[:], dt_s2[:], 1.0 / 17, None, ALU.mult)
                for odd in (15, 13, 11, 9, 7, 5, 3):
                    settle()
                    STT(dt_p[:], dt_p[:], 1.0 / odd, dt_s2[:], ALU.add, ALU.mult)
                settle()
                STT(dt_p[:], dt_p[:], 1.0, dt_s[:], ALU.add, ALU.mult)
                TS(dt_x[:], dt_x[:], 0.0, None, ALU.max)
                settle()
                STT(dt_rows[0:HEADS], dt_p[:], 2.0, dt_x[:], ALU.mult, ALU.add)
                settle()
                TS(dt_s[:], dt_rows[0:HEADS], a_neg[0:HEADS, 1:2], None, ALU.mult)
                settle()
                for t in range(TB):
                    c = slice(t * P, (t + 1) * P)
                    v.tensor_tensor_scan(dt_cum[:, c], dt_one[:, c], dt_s[:, c], 0.0, ALU.mult, ALU.add)
                settle()
                v.tensor_copy(acum[0:HEADS], dt_cum[:])
                TS(dt_rows[HEADS:2 * HEADS], dt_cum[:], -1.0, None, ALU.mult)
                for t in range(TB):
                    c = slice(t * P, (t + 1) * P)
                    TS(dt_rows[2 * HEADS:3 * HEADS, c], dt_cum[:, c], -1.0, dt_cum[:, (t + 1) * P - 1:(t + 1) * P],
                       ALU.mult, ALU.add)
                settle()
                TT(acum[HEADS:2 * HEADS], dt_cum[:], acum[0:HEADS].bitcast(F32), ALU.subtract)
                dve.drain().then_inc(S_["dt_v"], 1)

                def taps(step, nh, slot, j, block):
                    c = 2 * slot + j
                    dve.wait_ge(S_["seed"], step("seed") + 1)
                    for lag in range(1, CONV):
                        last = STT(conv[:, c, lag:S], gb[c][:, 0:S - lag],
                                   cw[:, bass.ds(block * CONV + (CONV - 1 - lag), 1)], conv[:, c, lag:S], ALU.mult, ALU.add)
                        if lag == CONV - 1:
                            last.then_inc(bank_free[slot], 1)
                        else:
                            settle()
                    dve.drain().then_inc(S_["taps"], 1)

                def silu(step, c, dst):
                    dve.wait_ge(S_["tanh"], step("tanh") + 1)
                    STT(dst, ctanh[:, c], 1.0, conv[:, c], ALU.add, ALU.mult).then_inc(S_["silu"], 1)

                def conv_round(step, base, block, dst):
                    for c in range(4):
                        taps(step, base, c // 2, c % 2, block + c)
                        if c % 2:
                            silu(step, c - 1, dst(c - 1))
                            silu(step, c, dst(c))

                with dve.Fori(0, N_BC // 2) as i:
                    conv_round(Step(l, "bc", i), i + U_BC // 2, i * 4,
                               lambda c: bct[:, bass.ds(i * 4 + c, 1), :].rearrange("p a n -> p (a n)"))

                def xs_round(i, first):
                    step = Step(l, "xs", i)
                    for c in range(4):
                        taps(step, i, c // 2, c % 2, i * 4 + (2 * N_BC + c))
                        for d in (c - 1, c) if c % 2 else ():
                            if not first:
                                dve.wait_ge(aux_full[d % 2], step.at(f"bank{d % 2}", d // 2 - 2) + 1)
                            silu(step, d, xsf[:, d])

                xs_round(0, True)
                with dve.Fori(1, N_XS // 2) as i:
                    xs_round(i, False)

                with dve.Fori(0, GROUPS) as g:
                    st = Step(l, "ssd", g)
                    yv = y_tok[:, :, bass.ds(g * GW, GW)]

                    def seg_sum(r):
                        b = full(st, 2 + r % 2)
                        TT(seg[:, r % 2], b[:].rearrange("p (t n) -> p t n", t=TB),
                           tok[:, :, bass.ds(g * HG + (HEADS + r), 1)].broadcast_to([P, TB, P]), ALU.add)\
                            .then_inc(aux_free[2 + r % 2], 1)
                        dve.drain().then_inc(S_["sum"], 1)

                    def masked(r):
                        dve.wait_ge(S_["seg"], st("seg") + 1)
                        dve.wait_ge(S_["m_used"], st.at("m_used", r - 2) + (1 + M_CREDIT))
                        TT(decayed[:, r % 2], seg[:, r % 2], cbm[:], ALU.mult).then_inc(S_["m"], 1)

                    seg_sum(0)
                    seg_sum(1)
                    st("bank0")
                    b = full(st, 0)
                    TT(cbm[:], b[:].rearrange("p (t n) -> p t n", t=TB),
                       con[:, K_TRI:K_TRI + P].unsqueeze(1).broadcast_to([P, TB, P]), ALU.mult).then_inc(aux_free[0], 1)
                    settle()
                    st("bank1")

                    def y_diag(r):
                        if r == 1:
                            dve.wait_ge(S_["dx"], st("dx") + 1)
                        b = full(st, 1)
                        dst = yv[:, :, (r - 1) * HD:(r + 1) * HD]
                        TT(dst, dst, b[:].rearrange("p (t n) -> p t n", t=TB), ALU.add).then_inc(aux_free[1], 1)

                    def heads(ap):
                        return ap.rearrange("p (h n) -> p h n", h=HG)

                    def next_state(t):
                        b = full(st, 0)
                        if t == 0:
                            v.tensor_copy(state[:, 0], b[:]).then_inc(aux_free[0], 1)
                        else:
                            TT(heads(state[:, t % 2]), heads(state[:, (t - 1) % 2]),
                               cdec[:, :, t:t + 1].broadcast_to([P, HG, HD]), ALU.mult)
                            settle()
                            TT(state[:, t % 2], state[:, t % 2], b[:], ALU.add).then_inc(aux_free[0], 1)
                        dve.drain().then_inc(S_["state"], 1)

                    def y_offset(t):
                        b = full(st, 0)
                        TT(heads(y_off[:]), heads(b[:]),
                           ea_tok[:, t, bass.ds(g * HG, HG)].unsqueeze(2).broadcast_to([P, HG, HD]), ALU.mult)\
                            .then_inc(aux_free[0], 1)
                        settle()
                        TT(yv[:, t, :], yv[:, t, :], y_off[:], ALU.add)
                        settle()

                    dve.wait_ge(S_["cdec"], st("cdec") + 1)
                    between = {0: (next_state, 0), 1: (y_offset, 1), 2: (next_state, 1), 3: (y_offset, 2),
                               4: (next_state, 2), 6: (y_offset, 3)}
                    for r in range(HG):
                        masked(r)
                        if r + 2 < HG:
                            seg_sum(r + 2)
                        if r % 2:
                            y_diag(r)
                        if r in between:
                            step, t = between[r]
                            step(t)

                v.memset(mix[:], 0.0)
                settle()

                def block_of(t, n):
                    return t[:, bass.ds(n, 1), :].rearrange("p a n -> p (a n)")

                with dve.Fori(0, 2) as i:
                    st = Step(l, "z", i)
                    def gate_y(u):
                        for j in range(2):
                            dve.wait_ge(S_["z_act"], st("z_act") + 1)
                            STT(zt[:], zt[:], 1.0, zh[:], ALU.add, ALU.mult)
                            settle()
                            yv = y_tok[:, 2 * j:2 * j + 2, bass.ds(i * (2 * GW) + u * UW, UW)]
                            TT(yv, yv, zt[:], ALU.mult)
                            dve.drain().then_inc(S_["z_used"], 1)

                    def y_low(gg, q):
                        dve.wait_ge(S_["y_hi"], st("y_hi") + 1)
                        STT(op_lo[:, 4 * gg + q, :], ab[q % 2][:], par[:, bass.ds(i * 8 + (C_SNG + 4 * gg + q), 1)],
                            op_hi[:, 4 * gg + q, :].bitcast(F32), ALU.mult, ALU.subtract).then_inc(aux_free[q % 2], 1)
                        dve.drain().then_inc(S_["y_lo"], 1)

                    for gg in range(2):
                        if gg == 0:
                            gate_y(0)
                            gate_y(1)
                        else:
                            gate_y(3)
                        dve.drain().then_inc(S_["y_gate"], 1)
                        dve.wait_ge(S_["y_sq"], st("y_sq") + 1)
                        TS(y_ms[:], y_ms[:], 1.0 / GW, EPS, ALU.mult, ALU.add).then_inc(S_["y_ms"], 1)
                        dve.wait_ge(S_["y_rs"], st("y_rs") + 1)
                        for q in range(4):
                            if q:
                                dve.wait_ge(aux_full[(q - 1) % 2], st.at(f"bank{(q - 1) % 2}", 2 * gg + (q - 1) // 2) + 1)
                            TT(yn[:], y_tok[:, :, bass.ds(i * (2 * GW) + (gg * GW + q * P), P)],
                               y_rs[:].unsqueeze(2).broadcast_to([P, TB, P]), ALU.mult).then_inc(S_["yn"], 1)
                            if q:
                                y_low(gg, q - 1)
                            if gg == 0 and q == 1:
                                gate_y(2)
                        y_low(gg, 3)
                    for u in range(4):
                        for j in range(2):
                            c = 2 * (u % 2) + j
                            dve.wait_ge(gemm_done, done_at(l, i * 8 + (U_ZS + 4 + u), j))
                            STT(zt[:].rearrange("p a n -> p (a n)"), gate_s[:, 2 * u + j, :], 1.0, gb[c][:], ALU.add, ALU.mult)\
                                .then_inc(bank_free[u % 2], 1)
                            settle()
                            TT(mix[:, 2 * u + j, :], mix[:, 2 * u + j, :], zt[:].rearrange("p a n -> p (a n)"), ALU.add)
                            settle()
                    dve.drain().then_inc(S_["z_used"], 1)

                st = Step(l, "att")
                dve.wait_ge(rope_in, (l + 1) * 32)

                def rope(pair, u):
                    n = 3 * pair + u
                    for j in range(2):
                        dve.wait_ge(S_["swap"], st("swap") + 1)
                        TT(qc[:], gb[2 * (n % 2) + j][:], rope_cos[:], ALU.mult).then_inc(bank_free[n % 2], 1)
                        TT(swap[:, j], swap[:, j], rope_sin[:], ALU.mult)
                        settle()
                        TT((qT, kT)[u][:, pair % 2, j, :], qc[:], swap[:, j], ALU.add)
                        dve.drain().then_inc(S_["rope"], 1)

                def maxima(j):
                    for part in range(2):
                        b = full(st, part)
                        TT(b[:, j * P:(j + 1) * P], b[:, j * P:(j + 1) * P], con[:, K_NEG:K_NEG + P], ALU.add)
                    settle()
                    for part in range(2):
                        v.tensor_reduce(mxs[:, part:part + 1], ab[part][:, 0:(j + 1) * P], AX_X, ALU.max)
                    settle()
                    TS(mxn[:, 2 * (j % 2):2 * (j % 2) + 2], mxs[:, 0:2], -(AD ** -0.5), None, ALU.mult)
                    dve.drain().then_inc(S_["mx"], 1)

                def difference(j):
                    dve.wait_ge(S_["e"], st("e") + 1)
                    d = slice(2 * (j % 2), 2 * (j % 2) + 2)
                    v.reciprocal(rden[:, d], den[:, d])
                    settle()
                    w = slice(0, (j + 1) * P)
                    d0, d1 = d.start, d.start + 1
                    TT(mxs[:, 2:3], rden[:, d1:d1 + 1], lams[:, 0:1], ALU.mult)
                    TS(probs[:, j % 2, 0, w], probs[:, j % 2, 0, w], rden[:, d0:d0 + 1], None, ALU.mult)
                    settle()
                    STT(probs[:, j % 2, 0, w], probs[:, j % 2, 1, w], mxs[:, 2:3], probs[:, j % 2, 0, w],
                        ALU.mult, ALU.add)
                    dve.drain().then_inc(S_["p"], 1)

                def o_norm():
                    dve.wait_ge(S_["o_sq"], st("o_sq") + 1)
                    TS(y_ms[:], y_ms[:], 1.0 / P, EPS, ALU.mult, ALU.add).then_inc(S_["o_ms"], 1)
                    dve.wait_ge(S_["o_rs"], st("o_rs") + 1)
                    TT(o_n[:], ab[3][:].rearrange("p (t n) -> p t n", t=TB),
                       y_rs[:].unsqueeze(2).broadcast_to([P, TB, P]), ALU.mult).then_inc(aux_free[3], 1)
                    dve.drain().then_inc(S_["on"], 1)

                def o_low(head):
                    dve.wait_ge(S_["o_hi"], st("o_hi") + 1)
                    STT(op_lo[:, head, :], ab[2][:], subg[:, 0:1], op_hi[:, head, :].bitcast(F32),
                        ALU.mult, ALU.subtract).then_inc(aux_free[2], 1)
                    dve.drain().then_inc(S_["o_lo"], 1)

                rope(0, 0)
                rope(0, 1)
                maxima(0)
                for n, (pair, h, j) in enumerate(ATT):
                    difference(j)
                    if n + 1 < len(ATT):
                        maxima(ATT[n + 1][2])
                    if n and n % TB == 0:
                        o_norm()
                    if n > TB and n % TB == 1:
                        o_low(n // TB - 1)
                    if pair + 1 < PAIRS and n % (2 * TB) in (3, 6):
                        rope(pair + 1, n % (2 * TB) // 3 - 1)
                o_norm()
                o_low(AH - 1)

                st = Step(l, "mix")
                for u in range(N_AO):
                    for j in range(2):
                        c = 2 * (u % 2) + j
                        dve.wait_ge(gemm_done, done_at(l, U_AO + u, j))
                        STT(zt[:].rearrange("p a n -> p (a n)"), gate_a[:, 2 * u + j, :], 1.0, gb[c][:], ALU.add, ALU.mult)\
                            .then_inc(bank_free[u % 2], 1)
                        settle()
                        TT(mix[:, 2 * u + j, :], mix[:, 2 * u + j, :], zt[:].rearrange("p a n -> p (a n)"), ALU.add)
                        settle()
                dve.drain().then_inc(S_["mixed"], 1)
                for k in range(KB):
                    dve.wait_ge(S_["mix_hi"], st("mix_hi") + 1)
                    TT(h_lo[:, k], mix[:, k], h_hi[:, k].bitcast(F32), ALU.subtract).then_inc(S_["mix_lo"], 1)
                dve.wait_ge(x_back, (l + 1) * 16)
                for u in range(N_WO):
                    for j in range(2):
                        dve.wait_ge(gemm_done, done_at(l, U_WO + u, j))
                        STT(x[:, 2 * u + j], gb[2 * (u % 2) + j][:], g1h[:, 2 * u + j:2 * u + j + 1], x[:, 2 * u + j],
                            ALU.mult, ALU.add).then_inc(bank_free[u % 2], 1)
                dve.drain().then_inc(S_["x_sum"], 1)
                norm_sums(st)
                norm(st, lambda k: amul[:, KB + k:KB + k + 1], lambda k: ada_v[:, 3, k:k + 1])

                with dve.Fori(0, 4) as i:
                    sf = Step(l, "ff", i)
                    for u in range(4):
                        for j in range(2):
                            c = 2 * (u % 2) + j
                            dve.wait_ge(S_["relu"], sf("relu") + 1)
                            TT(usq[:, j], relu[:, c], relu[:, c], ALU.mult)
                            settle()
                            dve.wait_ge(S_["u_hi"], sf("u_hi") + 1)
                            TT(op_lo[:, 2 * u + j, :], usq[:, j], op_hi[:, 2 * u + j, :].bitcast(F32), ALU.subtract)\
                                .then_inc(S_["u_lo"], 1)
                            settle()
                    for u in range(4):
                        for j in range(2):
                            dve.wait_ge(gemm_done, done_at(l, i * 8 + (U_FF + 4 + u), j))
                            STT(x[:, 2 * u + j], gb[2 * (u % 2) + j][:], ada_v[:, 5, 2 * u + j:2 * u + j + 1],
                                x[:, 2 * u + j], ALU.mult, ALU.add).then_inc(bank_free[u % 2], 1)
                    settle()
                dve.drain().then_inc(S_["layer"], 1)
            last_step = Step(DEPTH, "start")
            norm_sums(last_step)
            norm(last_step, lambda k: con[:, K_FG + k:K_FG + k + 1], None)

        def pool_program(pool):
            gp = nc.gpsimd

            def rsqrt(src, dst, step, want, give):
                pool.wait_ge(S_[want], step(want) + 1)
                gp.tensor_tensor(dst[:], src[:], half[:], ALU.pow).then_inc(S_[give], 1)

            def low(l, nh, slot):
                pool.wait_ge(hi_ready, l * UNITS + nh * 2 + (slot + 1))
                gp.tensor_tensor(w_lo[:, slot], raw[:, slot], w_hi[:, slot].bitcast(F32), ALU.subtract)\
                    .then_inc(lo_ready, 1)

            pool.sem_inc(lo_ready, LO_CREDIT)
            pool.sem_inc(ada_out, 2)
            pool.wait_ge(ready, 1)
            with pool.Fori(0, DEPTH) as l:
                st = Step(l, "start")
                rsqrt(ms, rs, st, "ms", "rs")
                low(l, 0, 0)
                low(l, 0, 1)
                with pool.Fori(1, U_GATE // 2 + 1) as i:
                    low(l, i, 0)
                    low(l, i, 1)
                with pool.Fori(0, GROUPS) as g:
                    st = Step(l, "ssd", g)
                    pool.wait_ge(S_["x_tok"], (l + 1) * TOTAL["x_tok"])
                    pool.wait_ge(S_["dt_a"], l * TOTAL["dt_a"] + 2)
                    pool.wait_ge(S_["m_used"], st.at("m_used", -HG) + HG + M_CREDIT)

                    def by_head(ap, c, t):
                        return ap[:, t, bass.ds(g * HG + c, HG)].unsqueeze(2).broadcast_to([P, HG, HD])

                    def heads(ap):
                        return ap.rearrange("p (h n) -> p h n", h=HG)

                    yv = y_tok[:, :, bass.ds(g * GW, GW)]
                    for t in range(TB):
                        gp.tensor_tensor(heads(xdt[:, t]), heads(yv[:, t, :]), by_head(tok, 0, t), ALU.mult)
                    pool.drain().then_inc(S_["xdt"], 1)
                    for t in range(TB - 1):
                        gp.tensor_tensor(heads(xd[:, t]), heads(xdt[:, t]), by_head(dec_tok, 0, t), ALU.mult)
                    pool.drain().then_inc(S_["xd"], 1)
                    skip = par[:, bass.ds(g * HG + C_DSK, HG)].unsqueeze(2).broadcast_to([P, HG, HD])
                    for t in range(TB):
                        gp.tensor_tensor(heads(yv[:, t, :]), heads(yv[:, t, :]), skip, ALU.mult)
                    pool.drain().then_inc(S_["dx"], 1)
                    low(l, g + (U_GATE // 2 + 1), 0)
                    low(l, g + (U_GATE // 2 + 1), 1)
                with pool.Fori(0, 2) as i:
                    st = Step(l, "z", i)
                    for gg in range(2):
                        for slot in range(2):
                            low(l, i * 4 + (U_ZS // 2 + gg + 1), slot)
                        rsqrt(y_ms, y_rs, st, "y_ms", "y_rs")
                    for u in range(4):
                        low(l, i * 4 + (U_ZS // 2 + 3 + u // 2), u % 2)
                st = Step(l, "att")

                def low_qkv(pair, u):
                    n = 3 * pair + u
                    low(l, U_QKV // 2 + n // 2 + 1, n % 2)

                for u in range(3):
                    low_qkv(0, u)
                for n, (pair, h, j) in enumerate(ATT):
                    if n and n % TB == 0:
                        rsqrt(y_ms, y_rs, st, "o_ms", "o_rs")
                    if pair + 1 < PAIRS and n % (2 * TB) in (2, 5, 7):
                        low_qkv(pair + 1, n % (2 * TB) // 3)
                rsqrt(y_ms, y_rs, st, "o_ms", "o_rs")
                st = Step(l, "mix")
                for nh in range(U_AO // 2 + 1, U_FF // 2 + 1):
                    low(l, nh, 0)
                    low(l, nh, 1)
                rsqrt(ms, rs, st, "ms", "rs")
                with pool.Fori(U_FF // 2 + 1, UNITS_H) as i:
                    low(l, i, 0)
                    low(l, i, 1)
            rsqrt(ms, rs, Step(DEPTH, "start"), "ms", "rs")

        block = ctx.enter_context(nc.Block())

        @block.sync
        def _(sp):
            sp_program(sp)

        @block.tensor
        def _(pe):
            pe_program(pe)

        @block.scalar
        def _(act):
            act_program(act)

        @block.vector
        def _(dve):
            dve_program(dve)

        @block.gpsimd
        def _(pool):
            pool_program(pool)


def _units(w):
    w = w.reshape(-1, KB, P, w.shape[1] // UW, UW)
    return w.transpose(0, 3, 2, 1, 4).reshape(-1, P, KB * UW)


def _blocks(v):
    return v.reshape(-1, P).T


def _layer_stream(a, l):
    w = a["w_in"][l]
    o = np.cumsum([0, DI, DI, 2 * GROUPS * STATE, HEADS, 2 * AH * AD, 2 * AH * AD, 2 * AH * AD, D, D])
    z, xs, bc, dt, q, k, v, gs, ga = (w[:, o[n]:o[n + 1]] for n in range(9))
    zu, so = _units(z), _units(a["w_ssm_out"][l])
    qu, ku, vu = _units(q), _units(k), _units(v)
    f1, f2 = _units(a["w_ff1"][l]), _units(a["w_ff2"][l])
    parts = [_units(a["w_ada"][l]), _units(bc), _units(xs), _units(gs), _units(ga)]
    for i in range(2):
        parts += [zu[4 * i:4 * i + 4], so[4 * i:4 * i + 4]]
    for p in range(4):
        parts += [qu[p:p + 1], ku[p:p + 1], vu[p:p + 1]]
    parts += [_units(a["w_attn_out"][l]), _units(a["w_out"][l])]
    for i in range(4):
        parts += [f1[4 * i:4 * i + 4], f2[4 * i:4 * i + 4]]
    dtw = np.zeros((P, KB, P), w.dtype)
    dtw[:, :, 0:HEADS] = dt.reshape(KB, P, HEADS).transpose(1, 0, 2)
    return np.concatenate(parts), dtw.reshape(P, KB * P)


def _layer_params(a, l):
    par = np.zeros((P, NPAR), np.float32)
    order = np.concatenate([np.arange(DI, DI + 2 * GROUPS * STATE), np.arange(DI)])
    par[:, C_N1:C_N1 + KB] = _blocks(a["norm1_g"][l])
    par[:, C_CW:C_CB] = a["conv_w"][l][:, order].reshape(CONV, CONV_BLOCKS, P).transpose(2, 1, 0).reshape(P, -1)
    par[:, C_CB:C_DSK] = _blocks(a["conv_b"][l][order])
    par[:, C_DSK:C_SNG] = a["d_skip"][l][None]
    par[:, C_SNG:C_SUB] = _blocks(a["ssm_norm_g"][l])
    par[:, C_SUB] = a["subln_g"][l]
    par[:, C_LAM:C_BADA] = np.concatenate([a[n][l] for n in ("lam_q1", "lam_k1", "lam_q2", "lam_k2")])[None]
    par[:, C_BADA:C_N2] = _blocks(a["b_ada"][l])
    par[:, C_N2:C_DTB] = _blocks(a["norm2_g"][l])
    par[0:HEADS, C_DTB] = a["dt_bias"][l]
    par[0:HEADS, C_ALOG] = a["a_log"][l]
    init = 0.8 - 0.6 * float(np.exp(-0.3 * l))
    par[:, C_LI], par[:, C_OML] = init, 1.0 - init
    return par


def _consts(a):
    con = np.zeros((P, NCON), np.float32)
    con[:, K_C:K_FG] = _blocks(a["c"][0])
    con[:, K_FG:K_ID] = _blocks(a["final_g"])
    con[:, K_ID:K_TRI] = np.eye(P)
    con[:, K_TRI:K_NEG] = np.triu(np.ones((P, P)))
    con[:, K_NEG:K_SEL] = np.where(np.tri(P) > 0, 0.0, -1e30)
    con[0:2 * HEADS, K_SEL:] = np.tile(np.eye(HEADS), (2, 1))
    inv = (1.0 / (np.float32(10000.0) ** (np.arange(0, AD, 2, dtype=np.float32) / np.float32(AD)))).astype(np.float32)
    ang = (np.arange(S, dtype=np.float32)[:, None] * inv[None, :]).astype(np.float32)
    cos, sin = np.cos(ang).T, np.sin(ang).T
    ropes = np.stack([np.tile(cos, (4, 1)), np.concatenate([-sin, sin, -sin, sin])]).astype(np.float32)
    return con, ropes


def kernel(**inputs):
    import concourse.bacc as bacc
    from concourse.bass_utils import run_bass_kernel_spmd

    a = {k: np.asarray(v) for k, v in inputs.items()}
    streams, dtws = zip(*(_layer_stream(a, l) for l in range(DEPTH)))
    con, ropes = _consts(a)
    arrays = {
        "stream": np.concatenate(streams),
        "dtw": np.stack(dtws),
        "params": np.stack([_layer_params(a, l) for l in range(DEPTH)]),
        "consts": con,
        "ropes": ropes,
        "xT": np.ascontiguousarray(a["x"][0].T.reshape(KB, P, S).transpose(1, 0, 2)),
    }
    nc = bacc.Bacc("TRN2", target_bir_lowering=False, num_devices=1)
    args = [nc.dram_tensor(n, v.shape, F32, kind="ExternalInput").ap() for n, v in arrays.items()]
    args.append(nc.dram_tensor("xsave", [P, KB, S], F32, kind="Internal").ap())
    args.append(nc.dram_tensor("out", [P, KB, S], F32, kind="ExternalOutput").ap())
    build(nc, *args)
    r = run_bass_kernel_spmd(nc, [arrays], core_ids=[0])
    y = r.results[0]["out"]
    return np.ascontiguousarray(y.transpose(1, 0, 2).reshape(D, S).T).reshape(1, S, D)
```
